# Optimizing a Trainium2 kernel written in Bass

```python
import math
import jax, jax.numpy as jnp
from jax import lax
import numpy as np

D_MODEL = 1024
BATCH = 1
SEQ = 256
DEPTH = 2

N_MIXERS = 2
N_CONV_LAYERS = (DEPTH + 1) // 2
N_ATTN_LAYERS = DEPTH // 2
D_FF = 2816
CONV_WIDTH = 31
DIFF_HEAD_DIM = 64
N_DIFF_HEADS = D_MODEL // (2 * DIFF_HEAD_DIM)
Q_BLOCK = 128
EPS = 1e-6

kernel_name = "hybrid_conformer_conv_diff_attn_macaron"

def _rmsnorm(x, g):
    xf = x.astype(jnp.float32)
    y = xf * lax.rsqrt(jnp.mean(xf * xf, axis=-1, keepdims=True) + EPS)
    return (y * g.astype(jnp.float32)).astype(x.dtype)

def _layernorm(x, g, b):
    xf = x.astype(jnp.float32)
    mu = jnp.mean(xf, axis=-1, keepdims=True)
    var = jnp.mean(jnp.square(xf - mu), axis=-1, keepdims=True)
    y = (xf - mu) * lax.rsqrt(var + EPS)
    return (y * g.astype(jnp.float32) + b.astype(jnp.float32)).astype(x.dtype)

def _swiglu_ffn(h, w_in, w_out):
    gu = h @ w_in
    gate, up = jnp.split(gu, 2, axis=-1)
    return (jax.nn.silu(gate) * up) @ w_out

def _conformer_conv(h, w_in, b_in, dw, dw_b, ln_g, ln_b, w_out, b_out):
    ab = h @ w_in + b_in
    a, b = jnp.split(ab, 2, axis=-1)
    u = a * jax.nn.sigmoid(b)
    u = lax.conv_general_dilated(
        u, dw[:, None, :].astype(u.dtype), window_strides=(1,),
        padding=[(CONV_WIDTH - 1, 0)],
        dimension_numbers=("NWC", "WIO", "NWC"),
        feature_group_count=D_MODEL) + dw_b
    u = _layernorm(u, ln_g, ln_b)
    u = jax.nn.silu(u)
    return u @ w_out + b_out

def _diff_attention(h, w_qkv, q_norm, k_norm, lq1, lk1, lq2, lk2, subln_g, w_out, layer_idx):
    B, S, _ = h.shape
    H, d = N_DIFF_HEADS, DIFF_HEAD_DIM
    lambda_init = 0.8 - 0.6 * math.exp(-0.3 * layer_idx)
    qkv = h @ w_qkv
    q, k, v = jnp.split(qkv, 3, axis=-1)
    q = _rmsnorm(q.reshape(B, S, H, 2, d), q_norm)
    k = _rmsnorm(k.reshape(B, S, H, 2, d), k_norm)
    v = v.reshape(B, S, H, 2 * d)
    q = jnp.transpose(q, (0, 2, 3, 1, 4)) * (1.0 / math.sqrt(d))
    k = jnp.transpose(k, (0, 2, 3, 1, 4))
    v = jnp.transpose(v, (0, 2, 1, 3))

    lam = (jnp.exp(jnp.sum(lq1.astype(jnp.float32) * lk1.astype(jnp.float32)))
           - jnp.exp(jnp.sum(lq2.astype(jnp.float32) * lk2.astype(jnp.float32)))
           + lambda_init)
    slopes = jnp.exp2(-8.0 * jnp.arange(1, H + 1, dtype=jnp.float32) / H)

    n_blk = S // Q_BLOCK
    q_blocks = jnp.moveaxis(q.reshape(B, H, 2, n_blk, Q_BLOCK, d), 3, 0)
    k_pos = jnp.arange(S)

    def block(args):
        qb, bi = args
        s = jnp.einsum("bhcqd,bhckd->bhcqk", qb, k).astype(jnp.float32)
        q_pos = bi * Q_BLOCK + jnp.arange(Q_BLOCK)
        dist = (q_pos[:, None] - k_pos[None, :]).astype(jnp.float32)
        bias = -slopes[:, None, None] * jnp.abs(dist)[None]
        s = jnp.where((dist >= 0)[None, None, None], s + bias[None, :, None], -jnp.inf)
        p = jax.nn.softmax(s, axis=-1)
        a = p[:, :, 0] - lam * p[:, :, 1]
        return jnp.einsum("bhqk,bhke->bhqe", a.astype(v.dtype), v)

    o = lax.map(block, (q_blocks, jnp.arange(n_blk)))
    o = jnp.transpose(o, (1, 0, 3, 2, 4)).reshape(B, S, H, 2 * d)
    o = _rmsnorm(o, subln_g) * (1.0 - lambda_init)
    return o.reshape(B, S, H * 2 * d) @ w_out

def setup_inputs(seed: int = 0) -> dict:
    key = jax.random.key(seed)
    ks = jax.random.split(key, 24)
    D, F, W, H, d = D_MODEL, D_FF, CONV_WIDTH, N_DIFF_HEADS, DIFF_HEAD_DIM
    NC, NA = N_CONV_LAYERS, N_ATTN_LAYERS
    nrm = lambda k, shape, s: jax.random.normal(k, shape, jnp.float32) * s
    gain = lambda k, shape: 1.0 + nrm(k, shape, 0.02)
    return {
        "x": nrm(ks[0], (BATCH, SEQ, D), 1.0),
        "ffn_norm": gain(ks[1], (DEPTH, 2, D)),
        "ffn_w_in": nrm(ks[2], (DEPTH, 2, D, 2 * F), D ** -0.5),
        "ffn_w_out": nrm(ks[3], (DEPTH, 2, F, D), F ** -0.5),
        "mix_norm": gain(ks[4], (DEPTH, D)),
        "conv_w_in": nrm(ks[5], (NC, D, 2 * D), D ** -0.5),
        "conv_b_in": nrm(ks[6], (NC, 2 * D), 0.02),
        "conv_dw": nrm(ks[7], (NC, W, D), W ** -0.5),
        "conv_dw_b": nrm(ks[8], (NC, D), 0.02),
        "conv_ln_g": gain(ks[9], (NC, D)),
        "conv_ln_b": nrm(ks[10], (NC, D), 0.02),
        "conv_w_out": nrm(ks[11], (NC, D, D), D ** -0.5),
        "conv_b_out": nrm(ks[12], (NC, D), 0.02),
        "attn_w_qkv": nrm(ks[13], (NA, D, 3 * D), D ** -0.5),
        "attn_q_norm": gain(ks[14], (NA, d)),
        "attn_k_norm": gain(ks[15], (NA, d)),
        "attn_lq1": nrm(ks[16], (NA, d), 0.1),
        "attn_lk1": nrm(ks[17], (NA, d), 0.1),
        "attn_lq2": nrm(ks[18], (NA, d), 0.1),
        "attn_lk2": nrm(ks[19], (NA, d), 0.1),
        "attn_subln_g": gain(ks[20], (NA, 2 * d)),
        "attn_w_out": nrm(ks[21], (NA, D, D), D ** -0.5),
    }

def reference(x, ffn_norm, ffn_w_in, ffn_w_out, mix_norm,
              conv_w_in, conv_b_in, conv_dw, conv_dw_b, conv_ln_g, conv_ln_b, conv_w_out, conv_b_out,
              attn_w_qkv, attn_q_norm, attn_k_norm, attn_lq1, attn_lk1, attn_lq2, attn_lk2,
              attn_subln_g, attn_w_out):
    for i in range(DEPTH):
        x = x + 0.5 * _swiglu_ffn(_rmsnorm(x, ffn_norm[i, 0]), ffn_w_in[i, 0], ffn_w_out[i, 0])
        h = _rmsnorm(x, mix_norm[i])
        j = i // N_MIXERS
        if i % N_MIXERS == 0:
            m = _conformer_conv(h, conv_w_in[j], conv_b_in[j], conv_dw[j], conv_dw_b[j],
                                conv_ln_g[j], conv_ln_b[j], conv_w_out[j], conv_b_out[j])
        else:
            m = _diff_attention(h, attn_w_qkv[j], attn_q_norm[j], attn_k_norm[j],
                                attn_lq1[j], attn_lk1[j], attn_lq2[j], attn_lk2[j],
                                attn_subln_g[j], attn_w_out[j], i)
        x = x + m
        x = x + 0.5 * _swiglu_ffn(_rmsnorm(x, ffn_norm[i, 1]), ffn_w_in[i, 1], ffn_w_out[i, 1])
    return x


_drawn_inputs = setup_inputs


def setup_inputs(seed=0):
    import zlib

    import numpy as np

    out = dict(_drawn_inputs(seed))
    spreads = {}
    factors = {'ffn_norm': 3.373,
     'mix_norm': 2.917,
     'conv_b_in': 3.73,
     'conv_ln_g': 3.484,
     'conv_ln_b': 3.742,
     'attn_q_norm': 7.459,
     'attn_k_norm': 7.827,
     'attn_subln_g': 6.488}
    for name, (base, spread) in spreads.items():
        noise = np.random.default_rng([zlib.crc32(name.encode()), seed]).standard_normal(out[name].shape)
        drawn = base * np.exp(spread * noise) if base else spread * noise
        out[name] = __import__('jax').numpy.asarray(drawn.astype(out[name].dtype))
    for name, factor in factors.items():
        out[name] = (out[name] * factor).astype(out[name].dtype)
    return out
```

```python
import math
from contextlib import ExitStack

import numpy as np
import concourse.bass as bass
from concourse import mybir

ALU = mybir.AluOpType
ACT = mybir.ActivationFunctionType
F32 = mybir.dt.float32
F32R = mybir.dt.float32r
AX_X = mybir.AxisListType.X

P = 128
D = 1024
T = 256
TT = T // P
KT = D // P
F = 2816
W = 31
PAD = W - 1
H = 8
DH = 64
EPS = 1e-6
DEPTH = 2
LAMBDA_INIT = 0.8 - 0.6 * math.exp(-0.3 * 1)
FAR = 1e36

CH = 256
FCH = F // CH
BANK = 512
UNIT = 2048
HALF = UNIT // 2
RAW = 3
RING = 6
AHEAD = 4
MIX = 7600

STAGES = [("ffn", 0, 0, FCH), ("conv", 0, 0, 2 * D // BANK), ("ffn", 0, 1, FCH),
          ("ffn", 1, 0, FCH), ("attn", 1, 0, 3 * D // BANK), ("ffn", 1, 1, FCH)]
SECOND = {"ffn": FCH, "conv": KT // 2, "attn": KT // 2}
UNIT0, CHUNK0, FFN0 = [], [], []
_u = _c = _f = 0
for _kind, _, _, _chunks in STAGES:
    UNIT0.append(_u)
    CHUNK0.append(_c)
    FFN0.append(_f)
    _u += 2 * _chunks + SECOND[_kind]
    _c += _chunks
    _f += _kind == "ffn"
UNITS = _u
CONV, ATTN = 1, 4
POWERS = [("turn", 0, 0), ("turn", 1, 0), ("ln", 0, 0), ("ln", 1, 0), ("turn", 2, 0), ("turn", 3, 0), ("turn", 4, 0)] \
    + [("qk", c, t) for c in range(4) for t in range(TT)] + [("out", 0, 0), ("out", 1, 0), ("turn", 5, 0)]
POWER_AT = {key: n for n, key in enumerate(POWERS)}
QK_CHUNKS = [0, 2, 1, 3, 4, 5]


def trunk(nc, x, ffn_norm, ffn_w_in, ffn_w_out, mix_norm, conv_w_in, conv_b_in, conv_dw, conv_dw_b,
          conv_ln_g, conv_ln_b, conv_w_out, conv_b_out, attn_w_qkv, attn_q_norm, attn_k_norm,
          attn_lq1, attn_lk1, attn_lq2, attn_lk2, attn_subln_g, attn_w_out, shape_consts, out):
    with ExitStack() as ctx:
        def sb(name, shape, dt=F32):
            return ctx.enter_context(nc.sbuf_tensor(name, shape, dt))

        def sem(name):
            return ctx.enter_context(nc.semaphore(name))

        raw = [sb(f"raw{i}", [P, UNIT]) for i in range(RAW)]
        w_hi = [sb(f"w_hi{i}", [P, UNIT], F32R) for i in range(RING)]
        w_lo = [sb(f"w_lo{i}", [P, UNIT], F32R) for i in range(RING)]
        xs = sb("xs", [P, TT, D])
        xg = sb("xg", [P, TT, D])
        gain = sb("gain", [P, 2, D])
        a_hi = sb("a_hi", [P, KT, T], F32R)
        a_lo = sb("a_lo", [P, KT, T], F32R)
        h_hi = sb("h_hi", [P, 2, 2, T], F32R)
        h_lo = sb("h_lo", [P, 2, 2, T], F32R)
        hs = sb("hs", [P, 2, TT, CH])
        hid, sil = hs[:, 0, :, :], hs[:, 1, :, :]
        junk = sb("junk", [P, 2, BANK], mybir.dt.bfloat16)
        consts = sb("consts", [P, P + 2 * P])
        ident = consts[:, 0:P]
        dist = consts[:, P:3 * P]
        ss = sb("ss", [P, 6, TT, 2])
        rstd = sb("rstd", [P, 6, TT])
        msq = sb("msq", [P, 6, TT])
        exponent = sb("exponent", [P, 8])
        mix = sb("mix", [P, MIX])

        acc = ctx.enter_context(nc.psum_tensor("acc", [P, 4, BANK], F32))
        pg = ctx.enter_context(nc.psum_tensor("pg", [P, 2, BANK], F32))
        pt = ctx.enter_context(nc.psum_tensor("pt", [P, 2, BANK], F32))

        at = 0
        ab = mix[:, at:at + TT * BANK].rearrange("p (t n) -> p t n", t=TT)
        at += TT * BANK
        sg = mix[:, at:at + TT * CH].rearrange("p (t n) -> p t n", t=TT)
        at += TT * CH
        up = mix[:, at:at + KT * (PAD + T)].rearrange("p (k n) -> p k n", k=KT)
        at += KT * (PAD + T)
        cv = mix[:, at:at + KT * T].rearrange("p (k n) -> p k n", k=KT)
        at += KT * T
        taps = mix[:, at:at + KT * W].rearrange("p (k w) -> p k w", k=KT)
        at += KT * W
        chan = mix[:, at:at + 3 * KT].rearrange("p (a k) -> p a k", a=3)
        at += 3 * KT
        b_out = mix[:, at:at + D]
        at += D
        bn = mix[:, at:at + 12].rearrange("p (a s) -> p a s", a=2)
        at += 12
        mv = mix[:, at:at + 2]
        at += 2
        ln_v, ln_r = mix[:, at:at + 1], mix[:, at + 1:at + 2]
        at += 2
        assert at <= MIX
        b_in = xg
        at = 0
        qT = mix[:, at:at + H * T].rearrange("p (h n) -> p h n", h=H)
        at += H * T
        kT = mix[:, at:at + H * T].rearrange("p (h n) -> p h n", h=H)
        at += H * T
        vv = mix[:, at:at + TT * D].rearrange("p (t n) -> p t n", t=TT)
        at += TT * D
        sc = mix[:, at:at + 2 * 2 * T].rearrange("p (s c n) -> p s c n", s=2, c=2)
        at += 2 * 2 * T
        aT = hs[:].rearrange("p a t n -> p (a t n)").rearrange("p (h n) -> p h n", h=H)
        small = mix[:, at:at + 400]
        at += 400
        assert at <= MIX
        gq = small[:, 0:2]
        gs = small[:, 2:3]
        lam4 = small[:, 4:4 + 4 * DH].rearrange("p (a d) -> p a d", a=4)
        lsum = small[:, 260:262]
        nlam = small[:, 262:263]
        grp = small[:, 264:280].rearrange("p (t g) -> p t g", t=TT)
        grr = small[:, 364:380].rearrange("p (t g) -> p t g", t=TT)
        mx = small[:, 280:284].rearrange("p (s c) -> p s c", s=2)
        sm = small[:, 284:288].rearrange("p (s c) -> p s c", s=2)
        rs = small[:, 288:292].rearrange("p (s c) -> p s c", s=2)
        lprod = small[:, 300:364]

        raw_ready = [sem(f"raw_ready{i}") for i in range(RAW)]
        hi_done = sem("hi_done")
        lo_done = sem("lo_done")
        unit_begun = sem("unit_begun")
        x_loaded = sem("x_loaded")
        consts_loaded = sem("consts_loaded")
        gain_loaded = [sem("gain_loaded0"), sem("gain_loaded1")]
        x_ready = sem("x_ready")
        xg_ready = sem("xg_ready")
        turned = sem("turned")
        a_hi_done = sem("a_hi_done")
        a_lo_done = sem("a_lo_done")
        ss_done = sem("ss_done")
        mean_done = sem("mean_done")
        power_done = sem("power_done")
        exponent_set = sem("exponent_set")
        chunk_done = sem("chunk_done")
        silu_done = sem("silu_done")
        chunk_out = sem("chunk_out")
        hid_turned = sem("hid_turned")
        h_hi_done = sem("h_hi_done")
        h_lo_done = sem("h_lo_done")
        acc_done = sem("acc_done")
        out_stored = sem("out_stored")
        step = sem("step")
        cv_loaded = sem("cv_loaded")
        bin_loaded = sem("bin_loaded")
        sig_done = sem("sig_done")
        ab_done = sem("ab_done")
        u_turned = sem("u_turned")
        pad_zero = sem("pad_zero")
        u_placed = sem("u_placed")
        tap_done = sem("tap_done")
        c_turned = sem("c_turned")
        ln_done = sem("ln_done")
        n_turned = sem("n_turned")
        act_done = sem("act_done")
        s_hi_done = sem("s_hi_done")
        s_lo_done = sem("s_lo_done")
        at_loaded = sem("at_loaded")
        lam_sum = sem("lam_sum")
        lam_exp = sem("lam_exp")
        sq_done = sem("sq_done")
        qn_done = sem("qn_done")
        q_turned = sem("q_turned")
        q_placed = sem("q_placed")
        sc_done = sem("sc_done")
        mx_done = sem("mx_done")
        ex_done = sem("ex_done")
        pr_done = sem("pr_done")
        p_turned = sem("p_turned")
        p_placed = sem("p_placed")
        o_done = sem("o_done")
        osq_done = sem("osq_done")
        on_done = sem("on_done")
        on_turned = sem("on_turned")
        o_hi_done = sem("o_hi_done")
        o_lo_done = sem("o_lo_done")

        block = ctx.enter_context(nc.Block())

        def w_in_source(s):
            kind, layer, which, _ = STAGES[s]
            if kind == "ffn":
                return ffn_w_in[layer, which].rearrange("(k p) n -> p k n", p=P), F
            if kind == "conv":
                return conv_w_in[0].rearrange("(k p) n -> p k n", p=P), D
            return attn_w_qkv[0].rearrange("(k p) n -> p k n", p=P), None

        def w_out_source(s):
            kind, layer, which, _ = STAGES[s]
            w = {"ffn": ffn_w_out[layer, which], "conv": conv_w_out[0], "attn": attn_w_out[0]}[kind]
            return w.rearrange("(k p) n -> p k n", p=P)

        @block.sync
        def _(sp):
            def slot_free(n, i):
                if n >= RAW:
                    sp.wait_ge(lo_done, 2 * (n - RAW + 1) + i * 2 * RING)

            def load_first(s, n, c, part, i=0):
                slot_free(n, i)
                src, apart = w_in_source(s)
                dst = raw[n % RAW][:].rearrange("p (k n) -> p k n", k=4)
                rows = slice(4 * part, 4 * part + 4)
                for g in range(2):
                    if apart is not None:
                        sp.dma_start(dst[:, :, g * CH:(g + 1) * CH],
                                     src[:, rows, bass.ds(c * CH + g * apart, CH)]).then_inc(raw_ready[n % RAW], 16)
                    else:
                        two = slice(4 * part + 2 * g, 4 * part + 2 * g + 2)
                        sp.dma_start(dst[:, 2 * g:2 * g + 2, :],
                                     src[:, two, bass.ds(QK_CHUNKS[c] * BANK, BANK)]).then_inc(raw_ready[n % RAW], 16)

            def load_second(s, n, c, i=0):
                slot_free(n, i)
                src = w_out_source(s)
                dst = raw[n % RAW][:].rearrange("p (k n) -> p k n", k=2)
                for g in range(2):
                    sp.dma_start(dst[:, g:g + 1, :], src[:, bass.ds(c * 2 + g, 1), :]).then_inc(raw_ready[n % RAW], 16)

            for t in range(TT):
                sp.dma_start(xs[:, t, :], x[0, t * P:(t + 1) * P, :]).then_inc(x_loaded, 16)
            for s, (kind, _, _, chunks) in enumerate(STAGES):
                u = UNIT0[s]
                if kind == "ffn":
                    load_first(s, u, 0, 0)
                    load_first(s, u + 1, 0, 1)

                    def chunk(c, i):
                        n = u + 2 + 3 * (c - 1)
                        load_first(s, n, i * 2 + c, 0, i)
                        load_first(s, n + 1, i * 2 + c, 1, i)
                        load_second(s, n + 2, i * 2 + (c - 1), i)

                    chunk(1, 0)
                    chunk(2, 0)
                    with sp.Fori(0, (FCH - 3) // 2) as i:
                        chunk(3, i)
                        chunk(4, i)
                    load_second(s, u + 32, FCH - 1)
                else:
                    for c in range(chunks):
                        load_first(s, u + 2 * c, c, 0)
                        load_first(s, u + 2 * c + 1, c, 1)
                    for c in range(KT // 2):
                        load_second(s, u + 2 * chunks + c, c)
            for half in range(2):
                for t in range(TT):
                    sp.wait_ge(x_ready, 4 * 5 + 2 * half + t + 1)
                    sp.dma_start(out[0, t * P:(t + 1) * P, half * BANK:(half + 1) * BANK],
                                 xs[:, t, half * BANK:(half + 1) * BANK]).then_inc(out_stored, 16)
            sp.wait_ge(out_stored, 16 * 4)

        @block.gpsimd
        def _(pool):
            gains = [ffn_norm[0, 0], mix_norm[0], ffn_norm[0, 1], ffn_norm[1, 0], mix_norm[1], ffn_norm[1, 1]]
            pool.dma_start(consts[:, :], shape_consts).then_inc(consts_loaded, 16)

            def load_gain(n):
                pool.dma_start(gain[:, n % 2, :], gains[n].partition_broadcast(P)).then_inc(gain_loaded[n % 2], 16)

            load_gain(0)
            load_gain(1)
            with nc.allow_non_contiguous_dma(reason="per-channel vectors, once"):
                for k in range(KT):
                    pool.dma_start(taps[:, k, :], conv_dw[0, :, k * P:(k + 1) * P].rearrange("w p -> p w")).then_inc(cv_loaded, 16)
                for a, v in enumerate((conv_dw_b, conv_ln_g, conv_ln_b)):
                    pool.dma_start(chan[:, a, :], v[0].rearrange("(k p) -> p k", p=P)).then_inc(cv_loaded, 16)
            pool.dma_start(b_out, conv_b_out[0].partition_broadcast(P)).then_inc(cv_loaded, 16)
            nc.gpsimd.memset(up[:, :, 0:PAD], 0.0).then_inc(pad_zero, 1)
            nc.gpsimd.memset(exponent[:, :], -0.5).then_inc(exponent_set, 1)
            pool.wait_ge(exponent_set, 1)
            for n, (kind, a, t) in enumerate(POWERS):
                src, dst = {"turn": lambda: (msq[:, a, :], rstd[:, a, :]), "ln": lambda: (ln_v, ln_r),
                            "qk": lambda: (grp[:, t, :], grr[:, t, :]), "out": lambda: (grp[:, a, :], grr[:, a, :])}[kind]()
                pool.wait_ge(mean_done, n + 1)
                nc.gpsimd.tensor_tensor(dst, src, exponent[:, 0:src.shape[-1]], ALU.pow).then_inc(power_done, 1)
                if kind == "turn" and a < 4:
                    pool.wait_ge(xg_ready, 4 * (a + 1))
                    load_gain(a + 2)
                if kind == "turn" and a == CONV:
                    pool.wait_ge(turned, 4 * (CONV + 1))
                    pool.dma_start(b_in[:].rearrange("p t n -> p (t n)"),
                                   conv_b_in[0].partition_broadcast(P)).then_inc(bin_loaded, 16)
                if kind == "turn" and a == CONV + 1:
                    pool.wait_ge(x_ready, 4 * (CONV + 1))
                    with nc.allow_non_contiguous_dma(reason="per-feature vectors, once"):
                        for c in range(2):
                            for b, v in enumerate((attn_q_norm, attn_k_norm)):
                                pool.dma_start(gq[c * DH:(c + 1) * DH, b:b + 1],
                                               v[0].rearrange("(d a) -> d a", a=1)).then_inc(at_loaded, 16)
                        pool.dma_start(gs, attn_subln_g[0].rearrange("(d a) -> d a", a=1)).then_inc(at_loaded, 16)
                    for b, v in enumerate((attn_lq1, attn_lk1, attn_lq2, attn_lk2)):
                        pool.dma_start(lam4[:, b, :], v[0].partition_broadcast(P)).then_inc(at_loaded, 16)

        @block.tensor
        def _(pe):
            def unit_ready(n, i=0):
                pe.wait_ge(lo_done, 2 * (n + 1) + i * 2 * RING)

            def products(dst, stat_hi, stat_lo, moves, first, last, begins, ends=None):
                for j, (m_hi, _) in enumerate(moves):
                    mm = pe.matmul(dst[j], stat_hi, m_hi, start=first, stop=False)
                    if begins and j == 0:
                        mm.then_inc(unit_begun, 1)
                for j, (_, m_lo) in enumerate(moves):
                    pe.matmul(dst[j], stat_hi, m_lo, start=False, stop=False)
                for j, (m_hi, _) in enumerate(moves):
                    mm = pe.matmul(dst[j], stat_lo, m_hi, start=False, stop=last)
                    if ends is not None:
                        mm.then_inc(ends, 1)

            def first_unit(n, part, banks, hooks=(), i=0):
                unit_ready(n, i)
                hi, lo = w_hi[n % RING], w_lo[n % RING]
                for k in range(4):
                    if k < len(hooks) and hooks[k] is not None:
                        hooks[k]()
                    kt = 4 * part + k
                    cols = slice(k * BANK, (k + 1) * BANK)
                    for t in range(TT):
                        tok = slice(t * P, (t + 1) * P)
                        end = kt == KT - 1
                        products([banks[t]], a_hi[:, kt, tok], a_lo[:, kt, tok], [(hi[:, cols], lo[:, cols])],
                                 kt == 0, end, k == 0 and t == 0, chunk_done if end else None)

            def second_unit(n, left, first, last, mid=None, i=0):
                unit_ready(n, i)
                hi, lo = w_hi[n % RING], w_lo[n % RING]

                def part(k, t, halves, end, begins):
                    s_hi, s_lo = left(k)
                    tok = slice(t * P, (t + 1) * P)
                    moves = [(hi[:, k * D + h * BANK:k * D + (h + 1) * BANK],
                              lo[:, k * D + h * BANK:k * D + (h + 1) * BANK]) for h in halves]
                    products([acc[:, 2 * t + h, :] for h in halves], s_hi[:, tok], s_lo[:, tok], moves,
                             first and k == 0, end, begins, acc_done if end else None)

                if last:
                    for h in range(2):
                        for t in range(TT):
                            for k in range(2):
                                part(k, t, (h,), k == 1, h == t == k == 0)
                else:
                    for k in range(2):
                        if k == 1 and mid is not None:
                            mid()
                        for t in range(TT):
                            part(k, t, (0, 1), False, t == k == 0)

            def turn(r, half):
                for t in range(TT):
                    pe.wait_ge(xg_ready, 4 * r + 2 * half + t + 1)
                    if half:
                        pe.wait_ge(a_lo_done, 4 * r + t + 1)
                    for k in range(4):
                        mm = pe.transpose(pt[:, t, k * P:(k + 1) * P],
                                          xg[:, t, half * BANK + k * P:half * BANK + (k + 1) * P], ident)
                    mm.then_inc(turned, 1)

            def a_ready(r, half):
                pe.wait_ge(a_lo_done, 4 * r + 2 * half + 2)

            def ffn(s):
                f, u, c0 = FFN0[s], UNIT0[s], CHUNK0[s]
                banks = [pg[:, t, :] for t in range(TT)]

                def banks_free(c, i=0):
                    pe.wait_ge(chunk_out, 2 * (c0 + c) + i * 4)

                def turn_hidden(c, i=0):
                    pe.wait_ge(chunk_out, 2 * (c0 + c + 1) + i * 4)
                    for k in range(2):
                        for t in range(TT):
                            mm = pe.transpose(pt[:, 0, (2 * k + t) * P:(2 * k + t + 1) * P],
                                              hid[:, t, k * P:(k + 1) * P], ident)
                    mm.then_inc(hid_turned, 1)

                def hidden_ready(c, i=0):
                    pe.wait_ge(h_lo_done, FCH * f + c + 1 + i * 2)

                def left(slot):
                    return lambda k: (h_hi[:, slot, k, :], h_lo[:, slot, k, :])

                turn(s, 0)
                a_ready(s, 0)
                first_unit(u, 0, banks, (None, None, lambda: turn(s, 1)))
                a_ready(s, 1)
                first_unit(u + 1, 1, banks)

                def chunk(c, b, i, first):
                    banks_free(c, i)
                    n = u + 2 + 3 * (c - 1)
                    first_unit(n, 0, banks, (None, None, lambda: turn_hidden(c - 1, 0)) if first else (), i)
                    first_unit(n + 1, 1, banks, (), i)
                    hidden_ready(c - 1, i)
                    second_unit(n + 2, left((c - 1) % 2), first, False, lambda: turn_hidden(c, i), i)

                chunk(1, 1, 0, True)
                chunk(2, 0, 0, False)
                with pe.Fori(0, (FCH - 3) // 2) as i:
                    chunk(3, 1, i, False)
                    chunk(4, 0, i, False)
                hidden_ready(FCH - 1)
                second_unit(u + 32, left((FCH - 1) % 2), False, True)

            def a_left(w):
                return lambda k: (a_hi[:, 2 * w + k, :], a_lo[:, 2 * w + k, :])

            def conv(s):
                u, c0 = UNIT0[s], CHUNK0[s]
                chunks = STAGES[s][3]

                def turn_u(c):
                    pe.wait_ge(chunk_out, 2 * (c0 + c + 1))
                    if c >= 2:
                        pe.wait_ge(u_placed, c - 1)
                    for k in range(2):
                        for t in range(TT):
                            mm = pe.transpose(pt[:, c % 2, (2 * k + t) * P:(2 * k + t + 1) * P],
                                              hid[:, t, k * P:(k + 1) * P], ident)
                    mm.then_inc(u_turned, 1)

                turn(s, 0)
                a_ready(s, 0)
                for c in range(chunks):
                    banks = [(acc if c % 2 else pg)[:, t, :] for t in range(TT)]
                    if c >= 2:
                        pe.wait_ge(chunk_out, 2 * (c0 + c - 1))
                    mid = (lambda: turn(s, 1)) if c == 0 else (lambda: turn_u(c - 1))
                    first_unit(u + 2 * c, 0, banks, (None, None, mid))
                    if c == 0:
                        a_ready(s, 1)
                    first_unit(u + 2 * c + 1, 1, banks)
                turn_u(chunks - 1)
                for t in range(TT):
                    for k in range(KT):
                        if t == 0:
                            pe.wait_ge(tap_done, 2 * W * (k // 2 + 1))
                        mm = pe.transpose(acc[:, 2 * t + k // 4, (k % 4) * P:(k % 4 + 1) * P],
                                          cv[:, k, t * P:(t + 1) * P], ident)
                    mm.then_inc(c_turned, 1)
                pe.wait_ge(u_placed, chunks)
                for j in range(KT // 2):
                    if j >= 2:
                        pe.wait_ge(act_done, j - 1)
                    for t in range(TT):
                        pe.wait_ge(ln_done, t + 1)
                        for k in range(2):
                            mm = pe.transpose(pt[:, j % 2, k * T + t * P:k * T + (t + 1) * P],
                                              xg[:, t, (2 * j + k) * P:(2 * j + k + 1) * P], ident)
                    mm.then_inc(n_turned, 1)
                for w in range(KT // 2):
                    pe.wait_ge(s_lo_done, w + 1)
                    second_unit(u + 2 * chunks + w, a_left(w), w == 0, w == KT // 2 - 1)

            def attn(s):
                u, c0 = UNIT0[s], CHUNK0[s]

                def turn_q(c):
                    for t in range(TT):
                        pe.wait_ge(qn_done, 2 * c + t + 1)
                        if c:
                            pe.wait_ge(q_placed, 2 * (c - 1) + t + 1)
                        for k in range(4):
                            mm = pe.transpose(pt[:, t, k * P:(k + 1) * P],
                                              xg[:, 0, t * BANK + k * P:t * BANK + (k + 1) * P], ident)
                        mm.then_inc(q_turned, 1)

                def scores(t, h):
                    n = t * H + h
                    keys = (t + 1) * P
                    if n >= 1:
                        pe.wait_ge(mx_done, n)
                    for c in range(2):
                        d = slice(c * DH, (c + 1) * DH)
                        mm = pe.matmul(acc[:, c, 0:keys], qT[d, h, t * P:(t + 1) * P], kT[d, h, 0:keys],
                                       start=True, stop=True)
                    mm.then_inc(sc_done, 1)

                def turn_p(t, h):
                    n = t * H + h
                    pe.wait_ge(pr_done, n + 1)
                    if n >= 2:
                        pe.wait_ge(p_placed, n - 1)
                    for b in range(t + 1):
                        mm = pe.transpose(pt[:, n % 2, b * P:(b + 1) * P], sc[:, n % 2, 0, b * P:(b + 1) * P], ident)
                    mm.then_inc(p_turned, 1)

                def values(t, h):
                    n = t * H + h
                    pe.wait_ge(p_placed, n + 1)
                    dst = pg[:, h // 4, (h % 4) * P:(h % 4 + 1) * P]
                    for b in range(t + 1):
                        left = aT[:, h, :] if t == 0 else aT[:, (n % 2) * 2 + b, :]
                        mm = pe.matmul(dst, left, vv[:, b, h * P:(h + 1) * P], start=b == 0, stop=b == t)
                    mm.then_inc(o_done, 1)

                turn(s, 0)
                a_ready(s, 0)
                for c in range(4):
                    banks = [(acc[:, 2 + t, :] if c % 2 else pg[:, t, :]) for t in range(TT)]
                    if c >= 2:
                        pe.wait_ge(chunk_out, 2 * (c0 + c - 1))
                    mid = (lambda: turn(s, 1)) if c == 0 else None
                    first_unit(u + 2 * c, 0, banks, (None, None, mid))
                    if c == 0:
                        a_ready(s, 1)
                    late = (lambda: turn_q(c - 1)) if c else None
                    first_unit(u + 2 * c + 1, 1, banks, (late,))
                for c in range(4, 6):
                    banks = [(acc[:, 2 + t, :] if c % 2 else pg[:, t, :]) for t in range(TT)]
                    pe.wait_ge(chunk_out, 2 * (c0 + c - 1))

                    def both(h):
                        if h == 0:
                            pe.wait_ge(q_placed, 8)
                        scores(0, h)
                        if h >= 1:
                            turn_p(0, h - 1)

                    if c == 4:
                        first_unit(u + 8, 0, banks, (None, None, lambda: turn_q(3)))
                        first_unit(u + 9, 1, banks, (None, lambda: both(0), None, lambda: both(1)))
                    else:
                        first_unit(u + 10, 0, banks, (None, lambda: both(2), None, lambda: both(3)))
                        first_unit(u + 11, 1, banks, (None, lambda: both(4), None, lambda: both(5)))
                both(6)
                both(7)
                scores(1, 0)
                turn_p(0, 7)
                pe.wait_ge(chunk_out, 2 * (c0 + 6))
                for h in range(H):
                    values(0, h)
                for h in range(1, H + 2):
                    if h < H:
                        scores(1, h)
                    if h <= H:
                        turn_p(1, h - 1)
                    if h >= 2:
                        if h == 2:
                            pe.wait_ge(on_done, 1)
                        values(1, h - 2)
                for t in range(TT):
                    for j in range(2):
                        pe.wait_ge(on_done, t + 1)
                        if t == 0:
                            pe.wait_ge(p_placed, 2 * H)
                        else:
                            pe.wait_ge(o_lo_done, j + 1)
                        for k in range(4):
                            mm = pe.transpose(pt[:, j, k * P:(k + 1) * P],
                                              xg[:, t, (4 * j + k) * P:(4 * j + k + 1) * P], ident)
                        mm.then_inc(on_turned, 1)
                for w in range(KT // 2):
                    pe.wait_ge(o_lo_done, 3 + w // 2)
                    second_unit(u + 12 + w, a_left(w), w == 0, w == KT // 2 - 1)

            pe.wait_ge(consts_loaded, 16)
            for s, (kind, _, _, _) in enumerate(STAGES):
                {"ffn": ffn, "conv": conv, "attn": attn}[kind](s)

        @block.scalar
        def _(act):
            def round_half(n, half, i=0):
                if half == 0:
                    act.wait_ge(raw_ready[n % RAW], 32 * (n // RAW + 1) + i * (32 * RING // RAW))
                    if n >= RING:
                        act.wait_ge(unit_begun, n - RING + 2 + i * RING)
                cols = slice(half * HALF, (half + 1) * HALF)
                nc.scalar.copy(w_hi[n % RING][:, cols], raw[n % RAW][:, cols]).then_inc(hi_done, 1)

            def tick(n, i=0, mid=None):
                if n + AHEAD < UNITS:
                    round_half(n + AHEAD, 0, i)
                if mid is not None:
                    mid()
                if n + AHEAD < UNITS:
                    round_half(n + AHEAD, 1, i)

            def turn(r, half):
                for t in range(TT):
                    act.wait_ge(turned, 4 * r + 2 * half + t + 1)
                    nc.scalar.copy(a_hi[:, 4 * half:4 * half + 4, t * P:(t + 1) * P],
                                   pt[:, t, :].rearrange("p (k n) -> p k n", k=4)).then_inc(a_hi_done, 1)
                for t in range(TT):
                    if r == 0:
                        act.wait_ge(x_loaded, 32)
                    else:
                        act.wait_ge(x_ready, 4 * (r - 1) + 2 * half + t + 1)
                    if 4 * r + 2 * half + t >= 2:
                        act.wait_ge(ss_done, 4 * r + 2 * half + t - 1)
                    nc.scalar.activation(junk[:, t, :], xs[:, t, half * BANK:(half + 1) * BANK], ACT.Square,
                                         accum_out=ss[:, r, t, half:half + 1]).then_inc(ss_done, 1)

            def ffn(s):
                f, u, c0 = FFN0[s], UNIT0[s], CHUNK0[s]

                def gate(c, i=0):
                    for t in range(TT):
                        act.wait_ge(chunk_done, 2 * (c0 + c) + t + 1 + i * 4)
                        nc.scalar.activation(sil[:, t, :], pg[:, t, 0:CH], ACT.Silu,
                                             scale=rstd[:, s, t:t + 1]).then_inc(silu_done, 1)

                def hidden(c, i=0):
                    act.wait_ge(hid_turned, FCH * f + c + 1 + i * 2)
                    nc.scalar.copy(h_hi[:, c % 2, :, :].rearrange("p k n -> p (k n)"), pt[:, 0, :]).then_inc(h_hi_done, 1)

                turn(s, 0)
                tick(u)
                turn(s, 1)
                tick(u + 1)
                act.wait_ge(power_done, POWER_AT["turn", s, 0] + 1)
                gate(0)
                tick(u + 2, 0, lambda: hidden(0))

                def chunk(c, i, skip_first):
                    n = u + 2 + 3 * (c - 1)
                    if not skip_first:
                        tick(n, i)
                    tick(n + 1, i)
                    gate(c, i)
                    tick(n + 2, i, lambda: hidden(c, i))

                chunk(1, 0, True)
                chunk(2, 0, False)
                peel = s == len(STAGES) - 1
                with act.Fori(0, (FCH - 3) // 2 - peel) as i:
                    chunk(3, i, False)
                    chunk(4, i, False)
                if peel:
                    chunk(FCH - 2, 0, False)
                    chunk(FCH - 1, 0, False)
                tick(u + 32)

            def conv(s):
                u, c0 = UNIT0[s], CHUNK0[s]
                chunks = STAGES[s][3]

                def place(c):
                    act.wait_ge(u_turned, c + 1)
                    nc.scalar.copy(up[:, 2 * c:2 * c + 2, PAD:PAD + T],
                                   pt[:, c % 2, :].rearrange("p (k n) -> p k n", k=2)).then_inc(u_placed, 1)

                turn(s, 0)
                tick(u)
                turn(s, 1)
                for c in range(chunks):
                    if c:
                        tick(u + 2 * c)
                    tick(u + 2 * c + 1)
                    for t in range(TT):
                        act.wait_ge(ab_done, 2 * c + t + 1)
                        nc.scalar.activation(sg[:, t, :], ab[:, t, CH:2 * CH], ACT.Sigmoid).then_inc(sig_done, 1)
                    if c:
                        place(c - 1)
                place(chunks - 1)
                tick(u + 2 * chunks)
                for j in range(KT // 2):
                    act.wait_ge(n_turned, j + 1)
                    for k in range(2):
                        kt = 2 * j + k
                        mm = nc.scalar.activation(cv[:, kt, :], pt[:, j % 2, k * T:(k + 1) * T], ACT.Silu,
                                                  bias=chan[:, 2, kt:kt + 1], scale=chan[:, 1, kt:kt + 1])
                    mm.then_inc(act_done, 1)
                    act.wait_ge(act_done, j + 1)
                    nc.scalar.copy(a_hi[:, 2 * j:2 * j + 2, :], cv[:, 2 * j:2 * j + 2, :]).then_inc(s_hi_done, 1)
                for w in range(1, 4):
                    tick(u + 2 * chunks + w)

            def attn(s):
                u, c0 = UNIT0[s], CHUNK0[s]

                def squares(c):
                    for t in range(TT):
                        act.wait_ge(chunk_out, 2 * (c0 + c) + t + 1)
                        nc.scalar.activation(xg[:, 1, t * BANK:(t + 1) * BANK], vv[:, t, 0:BANK],
                                             ACT.Square).then_inc(sq_done, 1)

                def place_q(c):
                    dst, a = (qT, 0) if c % 2 == 0 else (kT, 1)
                    if c == 0:
                        act.wait_ge(at_loaded, 16 * 9)
                    for t in range(TT):
                        act.wait_ge(q_turned, 2 * c + t + 1)
                        nc.scalar.activation(dst[:, 4 * (c // 2):4 * (c // 2) + 4, t * P:(t + 1) * P],
                                             pt[:, t, :].rearrange("p (k n) -> p k n", k=4), ACT.Copy,
                                             scale=gq[:, a:a + 1]).then_inc(q_placed, 1)

                def exps(n):
                    keys = (n // H + 1) * P
                    act.wait_ge(mx_done, n + 1)
                    for c in range(2):
                        mm = nc.scalar.activation(sc[:, n % 2, c, 0:keys], sc[:, n % 2, c, 0:keys], ACT.Exp,
                                                  bias=mx[:, n % 2, c:c + 1], accum_out=sm[:, n % 2, c:c + 1])
                    mm.then_inc(ex_done, 1)

                def place_p(n):
                    t, h = divmod(n, H)
                    act.wait_ge(p_turned, n + 1)
                    if t == 0:
                        nc.scalar.copy(aT[:, h, :], pt[:, n % 2, 0:P]).then_inc(p_placed, 1)
                    else:
                        act.wait_ge(o_done, H if h < 2 else H + h - 1)
                        b = (n % 2) * 2
                        nc.scalar.copy(aT[:, b:b + 2, :], pt[:, n % 2, 0:2 * P].rearrange("p (b n) -> p b n", b=2)).then_inc(p_placed, 1)

                turn(s, 0)
                tick(u)
                turn(s, 1)
                tick(u + 1)
                act.wait_ge(lam_sum, 1)
                nc.scalar.activation(lsum, lsum, ACT.Exp).then_inc(lam_exp, 1)
                squares(0)
                for c in range(1, 4):
                    tick(u + 2 * c)
                    tick(u + 2 * c + 1, 0, lambda: place_q(c - 1))
                    squares(c)
                tick(u + 8, 0, lambda: place_q(3))
                tick(u + 9)
                for n in range(H):
                    exps(n)
                    if n >= 1:
                        place_p(n - 1)
                    if n in (2, 4):
                        tick(u + 10 + (n == 4))
                exps(H)
                place_p(H - 1)
                for n in range(H + 1, 2 * H):
                    exps(n)
                    if n == H + 2:
                        act.wait_ge(o_done, H)
                        nc.scalar.activation(xg[:, 1, :], pg[:, :, :].rearrange("p a n -> p (a n)"), ACT.Square).then_inc(osq_done, 1)
                    place_p(n - 1)
                place_p(2 * H - 1)
                act.wait_ge(o_done, 2 * H)
                act.wait_ge(on_done, 1)
                nc.scalar.activation(xg[:, 1, :], pg[:, :, :].rearrange("p a n -> p (a n)"), ACT.Square).then_inc(osq_done, 1)
                tick(u + 12)
                for t in range(TT):
                    for j in range(2):
                        act.wait_ge(on_turned, 2 * t + j + 1)
                        nc.scalar.activation(a_hi[:, 4 * j:4 * j + 4, t * P:(t + 1) * P],
                                             pt[:, j, :].rearrange("p (k n) -> p k n", k=4), ACT.Copy,
                                             scale=gs).then_inc(o_hi_done, 1)
                for w in range(1, 4):
                    tick(u + 12 + w)

            for n in range(AHEAD):
                round_half(n, 0)
                round_half(n, 1)
            for s, (kind, _, _, _) in enumerate(STAGES):
                {"ffn": ffn, "conv": conv, "attn": attn}[kind](s)

        @block.vector
        def _(dve):
            links = [0]

            def link(ins):
                links[0] += 1
                ins.then_inc(step, 1)
                dve.wait_ge(step, links[0])

            def power_ready(*key):
                dve.wait_ge(power_done, POWER_AT[key] + 1)

            def rest_half(n, half, i=0):
                dve.wait_ge(hi_done, 2 * n + half + 1 + i * 2 * RING)
                cols = slice(half * HALF, (half + 1) * HALF)
                nc.vector.tensor_tensor(w_lo[n % RING][:, cols], raw[n % RAW][:, cols],
                                        w_hi[n % RING][:, cols].bitcast(F32), ALU.subtract).then_inc(lo_done, 1)

            def tick(n, i=0, mid=None):
                if n + AHEAD < UNITS:
                    rest_half(n + AHEAD, 0, i)
                if mid is not None:
                    mid()
                if n + AHEAD < UNITS:
                    rest_half(n + AHEAD, 1, i)

            def update(r, half, scale):
                cols = slice(half * BANK, (half + 1) * BANK)
                for t in range(TT):
                    if r:
                        dve.wait_ge(acc_done, 4 * (r - 1) + 2 * half + t + 1)
                        nc.vector.scalar_tensor_tensor(out=xs[:, t, cols], in0=acc[:, 2 * t + half, :], scalar=scale,
                                                       in1=xs[:, t, cols], op0=ALU.mult, op1=ALU.add).then_inc(x_ready, 1)
                    if r < len(STAGES):
                        if r:
                            dve.wait_ge(x_ready, 4 * (r - 1) + 2 * half + t + 1)
                        else:
                            dve.wait_ge(x_loaded, 32)
                        dve.wait_ge(gain_loaded[r % 2], 16 * (r // 2 + 1))
                        nc.vector.tensor_tensor(xg[:, t, cols], xs[:, t, cols], gain[:, r % 2, cols],
                                                ALU.mult).then_inc(xg_ready, 1)

            def turn_rest(r, half):
                for t in range(TT):
                    dve.wait_ge(a_hi_done, 4 * r + 2 * half + t + 1)
                    dst = (slice(None), slice(4 * half, 4 * half + 4), slice(t * P, (t + 1) * P))
                    nc.vector.tensor_tensor(a_lo[dst], pt[:, t, :].rearrange("p (k n) -> p k n", k=4),
                                            a_hi[dst].bitcast(F32), ALU.subtract).then_inc(a_lo_done, 1)

            def token_factors(r):
                dve.wait_ge(ss_done, 4 * (r + 1))
                link(nc.vector.tensor_tensor(msq[:, r, :], ss[:, r, :, 0], ss[:, r, :, 1], ALU.add))
                nc.vector.tensor_scalar(msq[:, r, :], msq[:, r, :], 1.0 / D, EPS, ALU.mult, ALU.add).then_inc(mean_done, 1)

            def enter(s, scale):
                update(s, 0, scale)
                turn_rest(s, 0)
                tick(UNIT0[s])
                update(s, 1, scale)
                turn_rest(s, 1)
                token_factors(s)

            def ffn(s):
                f, u, c0 = FFN0[s], UNIT0[s], CHUNK0[s]

                def gated(c, i=0):
                    for t in range(TT):
                        dve.wait_ge(silu_done, 2 * (FCH * f + c) + t + 1 + i * 4)
                        nc.vector.scalar_tensor_tensor(out=hid[:, t, :], in0=pg[:, t, CH:2 * CH],
                                                       scalar=rstd[:, s, t:t + 1], in1=sil[:, t, :],
                                                       op0=ALU.mult, op1=ALU.mult).then_inc(chunk_out, 1)

                def hidden(c, i=0):
                    dve.wait_ge(h_hi_done, FCH * f + c + 1 + i * 2)
                    nc.vector.tensor_tensor(h_lo[:, c % 2, :, :].rearrange("p k n -> p (k n)"), pt[:, 0, :],
                                            h_hi[:, c % 2, :, :].rearrange("p k n -> p (k n)").bitcast(F32),
                                            ALU.subtract).then_inc(h_lo_done, 1)

                tick(u + 1)
                power_ready("turn", s, 0)
                gated(0)
                tick(u + 2, 0, lambda: hidden(0))

                def chunk(c, i, skip_first):
                    n = u + 2 + 3 * (c - 1)
                    if not skip_first:
                        tick(n, i)
                    tick(n + 1, i)
                    gated(c, i)
                    tick(n + 2, i, lambda: hidden(c, i))

                chunk(1, 0, True)
                chunk(2, 0, False)
                peel = s == len(STAGES) - 1
                with dve.Fori(0, (FCH - 3) // 2 - peel) as i:
                    chunk(3, i, False)
                    chunk(4, i, False)
                if peel:
                    chunk(FCH - 2, 0, False)
                    chunk(FCH - 1, 0, False)
                tick(u + 32)

            def conv(s):
                u, c0 = UNIT0[s], CHUNK0[s]
                chunks = STAGES[s][3]

                def glu(c):
                    src = acc if c % 2 else pg
                    for t in range(TT):
                        dve.wait_ge(chunk_done, 2 * (c0 + c) + t + 1)
                        for g in range(2):
                            mm = nc.vector.scalar_tensor_tensor(
                                out=ab[:, t, g * CH:(g + 1) * CH], in0=src[:, t, g * CH:(g + 1) * CH],
                                scalar=rstd[:, s, t:t + 1],
                                in1=b_in[:].rearrange("p t n -> p (t n)")[:, g * D + c * CH:g * D + (c + 1) * CH],
                                op0=ALU.mult, op1=ALU.add)
                        mm.then_inc(ab_done, 1)
                    for t in range(TT):
                        dve.wait_ge(sig_done, 2 * c + t + 1)
                        nc.vector.tensor_tensor(hid[:, t, :], ab[:, t, 0:CH], sg[:, t, :], ALU.mult).then_inc(chunk_out, 1)

                def convolve(c):
                    dve.wait_ge(u_placed, c + 1)
                    for k in (2 * c, 2 * c + 1):
                        nc.vector.tensor_scalar(cv[:, k, :], up[:, k, 0:T], taps[:, k, 0:1], chan[:, 0, k:k + 1],
                                                ALU.mult, ALU.add).then_inc(tap_done, 1)
                    base = 2 * W * c
                    with dve.Fori(0, PAD // 2) as i:
                        for j in (1, 2):
                            for b, k in enumerate((2 * c, 2 * c + 1)):
                                dve.wait_ge(tap_done, base + 2 * (j - 1) + b + 1 + i * 4)
                                nc.vector.scalar_tensor_tensor(
                                    out=cv[:, k, :], in0=up[:, k, bass.ds(i * 2 + j, T)],
                                    scalar=taps[:, k, bass.ds(i * 2 + j, 1)], in1=cv[:, k, :],
                                    op0=ALU.mult, op1=ALU.add).then_inc(tap_done, 1)
                    dve.wait_ge(tap_done, base + 2 * W)

                dve.wait_ge(cv_loaded, 16 * (KT + 4))
                dve.wait_ge(bin_loaded, 16)
                dve.wait_ge(pad_zero, 1)
                power_ready("turn", s, 0)
                for c in range(chunks):
                    if c:
                        tick(u + 2 * c)
                    tick(u + 2 * c + 1)
                    glu(c)
                    if c:
                        convolve(c - 1)
                tick(u + 2 * chunks)
                convolve(chunks - 1)
                for t in range(TT):
                    nc.vector.tensor_tensor(xs[:, t, :], xs[:, t, :], b_out, ALU.add)
                for t in range(TT):
                    dve.wait_ge(c_turned, t + 1)
                    for a in range(2):
                        link(nc.vector.bn_stats(bn[:, a, :], acc[:, 2 * t + a, :]))
                    link(nc.vector.bn_aggr(mv, bn))
                    nc.vector.tensor_scalar(ln_v, mv[:, 1:2], EPS, None, ALU.add).then_inc(mean_done, 1)
                    power_ready("ln", t, 0)
                    nc.vector.tensor_scalar(xg[:, t, :], acc[:, 2 * t:2 * t + 2, :].rearrange("p a n -> p (a n)"),
                                            mv[:, 0:1], ln_r, ALU.subtract, ALU.mult).then_inc(ln_done, 1)
                for j in range(KT // 2):
                    dve.wait_ge(s_hi_done, j + 1)
                    nc.vector.tensor_tensor(a_lo[:, 2 * j:2 * j + 2, :], cv[:, 2 * j:2 * j + 2, :],
                                            a_hi[:, 2 * j:2 * j + 2, :].bitcast(F32), ALU.subtract).then_inc(s_lo_done, 1)
                for w in range(1, 4):
                    tick(u + 2 * chunks + w)

            def attn(s):
                u, c0 = UNIT0[s], CHUNK0[s]

                def lambdas():
                    dve.wait_ge(at_loaded, 16 * 9)
                    for a in range(2):
                        link(nc.vector.tensor_tensor(lprod, lam4[:, 2 * a, :], lam4[:, 2 * a + 1, :], ALU.mult))
                        mm = nc.vector.reduce_sum(lsum[:, a:a + 1], lprod, AX_X)
                        if a == 0:
                            link(mm)
                    mm.then_inc(lam_sum, 1)

                def take(c):
                    src = [(acc[:, 2 + t, :] if c % 2 else pg[:, t, :]) for t in range(TT)]
                    for t in range(TT):
                        dve.wait_ge(chunk_done, 2 * (c0 + c) + t + 1)
                        cols = slice(0, BANK) if c < 4 else slice((c - 4) * BANK, (c - 3) * BANK)
                        nc.vector.tensor_scalar(vv[:, t, cols], src[t], rstd[:, s, t:t + 1], None,
                                                ALU.mult).then_inc(chunk_out, 1)

                def norm_qk(c):
                    under = float(DH) if c % 2 == 0 else 1.0
                    for t in range(TT):
                        dve.wait_ge(sq_done, 2 * c + t + 1)
                        link(nc.vector.reduce_sum(grp[:, t, :], xg[:, 1, t * BANK:(t + 1) * BANK].rearrange("p (g d) -> p g d", d=DH), AX_X))
                        nc.vector.tensor_scalar(grp[:, t, :], grp[:, t, :], under / DH, under * EPS,
                                                ALU.mult, ALU.add).then_inc(mean_done, 1)
                        power_ready("qk", c, t)
                        if c:
                            dve.wait_ge(q_turned, 2 * (c - 1) + t + 1)
                        nc.vector.tensor_tensor(xg[:, 0, t * BANK:(t + 1) * BANK].rearrange("p (g d) -> p g d", d=DH),
                                                vv[:, t, 0:BANK].rearrange("p (g d) -> p g d", d=DH),
                                                grr[:, t, :].rearrange("p (g a) -> p g a", a=1).to_broadcast([P, BANK // DH, DH]),
                                                ALU.mult).then_inc(qn_done, 1)

                def biased(n):
                    t, h = divmod(n, H)
                    keys = (t + 1) * P
                    slope = 2.0 ** (-8.0 * (h + 1) / H)
                    dve.wait_ge(sc_done, n + 1)
                    if n >= 2:
                        dve.wait_ge(p_turned, n - 1)
                    d = dist[:, 2 * P - keys:2 * P].rearrange("p (a n) -> p a n", a=1).to_broadcast([P, 2, keys])
                    link(nc.vector.scalar_tensor_tensor(out=sc[:, n % 2, :, 0:keys], in0=d, scalar=-slope,
                                                        in1=acc[:, 0:2, 0:keys], op0=ALU.mult, op1=ALU.add))
                    link(nc.vector.reduce_max(mx[:, n % 2, :], sc[:, n % 2, :, 0:keys], AX_X))
                    nc.vector.tensor_scalar(mx[:, n % 2, :], mx[:, n % 2, :], -1.0, None, ALU.mult).then_inc(mx_done, 1)

                def combined(n):
                    keys = (n // H + 1) * P
                    dve.wait_ge(ex_done, n + 1)
                    link(nc.vector.reciprocal(rs[:, n % 2, :], sm[:, n % 2, :]))
                    link(nc.vector.tensor_tensor(rs[:, n % 2, 1:2], rs[:, n % 2, 1:2], nlam, ALU.mult))
                    link(nc.vector.tensor_scalar(sc[:, n % 2, 0, 0:keys], sc[:, n % 2, 0, 0:keys],
                                                 rs[:, n % 2, 0:1], None, ALU.mult))
                    nc.vector.scalar_tensor_tensor(out=sc[:, n % 2, 0, 0:keys], in0=sc[:, n % 2, 1, 0:keys],
                                                   scalar=rs[:, n % 2, 1:2], in1=sc[:, n % 2, 0, 0:keys],
                                                   op0=ALU.mult, op1=ALU.add).then_inc(pr_done, 1)

                def norm_out(t):
                    dve.wait_ge(osq_done, t + 1)
                    g = grp[:, t, :]
                    link(nc.vector.reduce_sum(g, xg[:, 1, :].rearrange("p (g d) -> p g d", g=H), AX_X))
                    under = (1.0 - LAMBDA_INIT) ** -2
                    nc.vector.tensor_scalar(g, g, under / (2 * DH), under * EPS, ALU.mult, ALU.add).then_inc(mean_done, 1)
                    power_ready("out", t, 0)
                    nc.vector.tensor_tensor(xg[:, t, :].rearrange("p (g d) -> p g d", g=H),
                                            pg[:, :, :].rearrange("p a (g d) -> p (a g) d", d=P),
                                            grr[:, t, :].rearrange("p (g a) -> p g a", a=1).to_broadcast([P, H, P]),
                                            ALU.mult).then_inc(on_done, 1)

                lambdas()
                tick(u + 1)
                power_ready("turn", s, 0)
                take(0)
                for c in range(1, 4):
                    norm_qk(c - 1)
                    tick(u + 2 * c)
                    tick(u + 2 * c + 1)
                    take(c)
                dve.wait_ge(lam_exp, 1)
                link(nc.vector.tensor_tensor(nlam, lsum[:, 1:2], lsum[:, 0:1], ALU.subtract))
                link(nc.vector.tensor_scalar(nlam, nlam, -LAMBDA_INIT, None, ALU.add))
                norm_qk(3)
                tick(u + 8)
                tick(u + 9)
                biased(0)
                for n in range(1, H):
                    biased(n)
                    combined(n - 1)
                    if n == 1:
                        take(4)
                    if n in (3, 5):
                        tick(u + 10 + (n == 5))
                take(5)
                biased(H)
                combined(H - 1)
                for n in range(H + 1, 2 * H):
                    biased(n)
                    combined(n - 1)
                    if n == H + 2:
                        norm_out(0)
                combined(2 * H - 1)
                norm_out(1)
                tick(u + 12)
                for t in range(TT):
                    for j in range(2):
                        dve.wait_ge(o_hi_done, 2 * t + j + 1)
                        dst = (slice(None), slice(4 * j, 4 * j + 4), slice(t * P, (t + 1) * P))
                        nc.vector.scalar_tensor_tensor(out=a_lo[dst], in0=pt[:, j, :].rearrange("p (k n) -> p k n", k=4),
                                                       scalar=gs, in1=a_hi[dst].bitcast(F32), op0=ALU.mult,
                                                       op1=ALU.subtract).then_inc(o_lo_done, 1)
                for w in range(1, 4):
                    tick(u + 12 + w)

            for n in range(AHEAD):
                rest_half(n, 0)
                rest_half(n, 1)
            for s, (kind, _, _, _) in enumerate(STAGES):
                enter(s, 0.5 if s and STAGES[s - 1][0] == "ffn" else 1.0)
                {"ffn": ffn, "conv": conv, "attn": attn}[kind](s)
            update(len(STAGES), 0, 0.5)
            update(len(STAGES), 1, 0.5)


NAMES = ["x", "ffn_norm", "ffn_w_in", "ffn_w_out", "mix_norm", "conv_w_in", "conv_b_in", "conv_dw", "conv_dw_b",
         "conv_ln_g", "conv_ln_b", "conv_w_out", "conv_b_out", "attn_w_qkv", "attn_q_norm", "attn_k_norm",
         "attn_lq1", "attn_lk1", "attn_lq2", "attn_lk2", "attn_subln_g", "attn_w_out"]


def kernel(**inputs):
    import concourse.bacc as bacc
    from concourse.bass_utils import run_bass_kernel_spmd as run

    nc = bacc.Bacc("TRN2", target_bir_lowering=False, num_devices=1)
    arrays, args = {}, []
    for name in NAMES:
        a = np.ascontiguousarray(inputs[name])
        arrays[f"in_{name}"] = a
        args.append(nc.dram_tensor(f"in_{name}", a.shape, mybir.dt.from_np(a.dtype), kind="ExternalInput").ap())
    away = np.arange(P)[:, None] + P - np.arange(2 * P)[None, :]
    consts = np.concatenate([np.eye(P), np.where(away < 0, FAR, away)], axis=1).astype(np.float32)
    arrays["in_consts"] = consts
    args.append(nc.dram_tensor("in_consts", consts.shape, F32, kind="ExternalInput").ap())
    y = nc.dram_tensor("out_y", (1, T, D), F32, kind="ExternalOutput").ap()
    trunk(nc, *args, y)
    return run(nc, [arrays], core_ids=[0]).results[0]["out_y"]
```

```python
import math
from contextlib import ExitStack

import numpy as np
import concourse.bass as bass
from concourse import mybir

ALU = mybir.AluOpType
ACT = mybir.ActivationFunctionType
F32 = mybir.dt.float32
F32R = mybir.dt.float32r
AX_X = mybir.AxisListType.X

P = 128
D = 1024
T = 256
TT = T // P
KT = D // P
F = 2816
W = 31
PAD = W - 1
H = 8
DH = 64
EPS = 1e-6
DEPTH = 2
LAMBDA_INIT = 0.8 - 0.6 * math.exp(-0.3 * 1)
FAR = 1e36

CH = 256
FCH = F // CH
BANK = 512
UNIT = 2048
HALF = UNIT // 2
RAW = 3
RING = 6
AHEAD = 4
MIX = 7600
VK = 4
PK = KT - VK
DIAGS = 5
ROWS = W + 3
HEAD, STEP, TAIL = 3, DIAGS, 3

STAGES = [("ffn", 0, 0, FCH), ("conv", 0, 0, 2 * D // BANK), ("ffn", 0, 1, FCH),
          ("ffn", 1, 0, FCH), ("attn", 1, 0, 3 * D // BANK), ("ffn", 1, 1, FCH)]
SECOND = {"ffn": FCH, "conv": KT // 2, "attn": KT // 2}
UNIT0, CHUNK0, FFN0 = [], [], []
_u = _c = _f = 0
for _kind, _, _, _chunks in STAGES:
    UNIT0.append(_u)
    CHUNK0.append(_c)
    FFN0.append(_f)
    _u += 2 * _chunks + SECOND[_kind]
    _c += _chunks
    _f += _kind == "ffn"
UNITS = _u
CONV, ATTN = 1, 4
POWERS = [("turn", 0, 0), ("turn", 1, 0), ("ln", 0, 0), ("turn", 2, 0), ("turn", 3, 0), ("turn", 4, 0)] \
    + [("qk", c, t) for c in range(4) for t in range(TT)] + [("out", 0, 0), ("out", 1, 0), ("turn", 5, 0)]
POWER_AT = {key: n for n, key in enumerate(POWERS)}
QK_CHUNKS = [0, 2, 1, 3, 4, 5]


def trunk(nc, x, ffn_norm, ffn_w_in, ffn_w_out, mix_norm, conv_w_in, conv_b_in, conv_dw, conv_dw_b,
          conv_ln_g, conv_ln_b, conv_w_out, conv_b_out, attn_w_qkv, attn_q_norm, attn_k_norm,
          attn_lq1, attn_lk1, attn_lq2, attn_lk2, attn_subln_g, attn_w_out, shape_consts, out):
    with ExitStack() as ctx:
        def sb(name, shape, dt=F32):
            return ctx.enter_context(nc.sbuf_tensor(name, shape, dt))

        def sem(name):
            return ctx.enter_context(nc.semaphore(name))

        raw = [sb(f"raw{i}", [P, UNIT]) for i in range(RAW)]
        w_hi = [sb(f"w_hi{i}", [P, UNIT], F32R) for i in range(RING)]
        w_lo = [sb(f"w_lo{i}", [P, UNIT], F32R) for i in range(RING)]
        xs = sb("xs", [P, TT, D])
        xg = sb("xg", [P, TT, D])
        gain = sb("gain", [P, 2, D])
        a_hi = sb("a_hi", [P, KT, T], F32R)
        a_lo = sb("a_lo", [P, KT, T], F32R)
        h_hi = sb("h_hi", [P, 2, 2, T], F32R)
        h_lo = sb("h_lo", [P, 2, 2, T], F32R)
        hs = sb("hs", [P, 2, TT, CH])
        hid, sil = hs[:, 0, :, :], hs[:, 1, :, :]
        junk = sb("junk", [P, 2, BANK], mybir.dt.bfloat16)
        consts = sb("consts", [P, P + 2 * P])
        ident = consts[:, 0:P]
        dist = consts[:, P:3 * P]
        ss = sb("ss", [P, 6, TT, 2])
        rstd = sb("rstd", [P, 6, TT])
        msq = sb("msq", [P, 6, TT])
        exponent = sb("exponent", [P, 8])
        more_diags = sb("more_diags", [P, 2, DIAGS - 3, P], F32R)
        mix = sb("mix", [P, MIX])

        acc = ctx.enter_context(nc.psum_tensor("acc", [P, 4, BANK], F32))
        pg = ctx.enter_context(nc.psum_tensor("pg", [P, 2, BANK], F32))
        pt = ctx.enter_context(nc.psum_tensor("pt", [P, 2, BANK], F32))

        at = 0
        ab = mix[:, at:at + TT * BANK].rearrange("p (t n) -> p t n", t=TT)
        at += TT * BANK
        sg = sil
        up = mix[:, at:at + VK * (PAD + T)].rearrange("p (k n) -> p k n", k=VK)
        at += VK * (PAD + T)
        cv = mix[:, at:at + KT * T].rearrange("p (k n) -> p k n", k=KT)
        at += KT * T
        rows = cv[:].rearrange("p k n -> p (k n)")[0:ROWS, 0:D]
        chan = mix[:, at:at + KT * ROWS].rearrange("p (k w) -> p k w", k=KT)
        at += KT * ROWS
        tap_hi = mix[:, at:at + PK * W].rearrange("p (k w) -> p k w", k=PK).bitcast(F32R)
        at += PK * W
        tap_lo = mix[:, at:at + PK * W].rearrange("p (k w) -> p k w", k=PK)
        at += PK * W
        b_out = mix[:, at:at + D]
        at += D
        bn = mix[:, at:at + 24].rearrange("p (t a s) -> p t a s", t=TT, a=2)
        at += 24
        mv = mix[:, at:at + 4].rearrange("p (t a) -> p t a", t=TT)
        at += 4
        ln_v, ln_r, ln_b = mix[:, at:at + 2], mix[:, at + 2:at + 4], mix[:, at + 4:at + 5]
        at += 5
        warm = mix[:, at:at + 1]
        at += 1
        in_h = [h[:].rearrange("p a k n -> p (a k n)") for h in (h_hi, h_lo)]
        up_hi, up_lo = (h[:, 0:2 * (PAD + T)].rearrange("p (k n) -> p k n", k=2) for h in in_h)

        def diag(part, d):
            slot, here = d % DIAGS, 3
            at = 2 * (PAD + T) + slot * P
            return in_h[part][:, at:at + P] if slot < here else more_diags[:, part, slot - here, :]
        assert at <= MIX
        b_in = xg
        at = 0
        qT = mix[:, at:at + H * T].rearrange("p (h n) -> p h n", h=H)
        at += H * T
        kT = mix[:, at:at + H * T].rearrange("p (h n) -> p h n", h=H)
        at += H * T
        vv = mix[:, at:at + TT * D].rearrange("p (t n) -> p t n", t=TT)
        at += TT * D
        sc = mix[:, at:at + 2 * 2 * T].rearrange("p (s c n) -> p s c n", s=2, c=2)
        at += 2 * 2 * T
        aT = hs[:].rearrange("p a t n -> p (a t n)").rearrange("p (h n) -> p h n", h=H)
        small = mix[:, at:at + 400]
        at += 400
        assert at <= MIX
        gq = small[:, 0:2]
        gs = small[:, 2:3]
        lam4 = small[:, 4:4 + 4 * DH].rearrange("p (a d) -> p a d", a=4)
        lsum = small[:, 260:262]
        nlam = small[:, 262:263]
        grp = small[:, 264:280].rearrange("p (t g) -> p t g", t=TT)
        grr = small[:, 364:380].rearrange("p (t g) -> p t g", t=TT)
        mx = small[:, 280:284].rearrange("p (s c) -> p s c", s=2)
        sm = small[:, 284:288].rearrange("p (s c) -> p s c", s=2)
        rs = small[:, 288:292].rearrange("p (s c) -> p s c", s=2)
        lprod = small[:, 300:364]

        raw_ready = [sem(f"raw_ready{i}") for i in range(RAW)]
        hi_done = sem("hi_done")
        lo_done = sem("lo_done")
        unit_begun = sem("unit_begun")
        x_loaded = sem("x_loaded")
        consts_loaded = sem("consts_loaded")
        gain0_loaded = sem("gain0_loaded")
        gain_loaded = [sem("gain_loaded0"), sem("gain_loaded1")]
        x_ready = sem("x_ready")
        xg_ready = sem("xg_ready")
        turned = sem("turned")
        a_hi_done = sem("a_hi_done")
        a_lo_done = sem("a_lo_done")
        ss_done = sem("ss_done")
        mean_done = sem("mean_done")
        power_done = sem("power_done")
        exponent_set = sem("exponent_set")
        chunk_done = sem("chunk_done")
        silu_done = sem("silu_done")
        chunk_out = sem("chunk_out")
        hid_turned = sem("hid_turned")
        h_hi_done = sem("h_hi_done")
        h_lo_done = sem("h_lo_done")
        acc_done = sem("acc_done")
        out_stored = sem("out_stored")
        step = sem("step")
        rows_loaded = sem("rows_loaded")
        rows_turned = sem("rows_turned")
        chan_set = sem("chan_set")
        tap_lo_set = sem("tap_lo_set")
        b_out_loaded = sem("b_out_loaded")
        up_lo_set = sem("up_lo_set")
        diag_hi_set = sem("diag_hi_set")
        diag_lo_set = sem("diag_lo_set")
        diag_used = sem("diag_used")
        cv_taken = sem("cv_taken")
        bin_loaded = sem("bin_loaded")
        sig_done = sem("sig_done")
        ab_done = sem("ab_done")
        u_turned = sem("u_turned")
        pad_zero = sem("pad_zero")
        u_placed = sem("u_placed")
        tap_done = sem("tap_done")
        c_turned = sem("c_turned")
        ln_b_set = sem("ln_b_set")
        ln_done = [sem(f"ln_done{t}") for t in range(TT)]
        n_turned = sem("n_turned")
        act_done = sem("act_done")
        s_hi_done = sem("s_hi_done")
        s_lo_done = sem("s_lo_done")
        at_loaded = sem("at_loaded")
        lam_sum = sem("lam_sum")
        lam_exp = sem("lam_exp")
        sq_done = sem("sq_done")
        qn_done = sem("qn_done")
        q_turned = sem("q_turned")
        q_placed = sem("q_placed")
        sc_done = sem("sc_done")
        mx_done = sem("mx_done")
        ex_done = sem("ex_done")
        pr_done = sem("pr_done")
        p_turned = sem("p_turned")
        p_placed = sem("p_placed")
        o_done = sem("o_done")
        osq_done = sem("osq_done")
        on_done = sem("on_done")
        on_turned = sem("on_turned")
        o_hi_done = sem("o_hi_done")
        o_lo_done = sem("o_lo_done")

        block = ctx.enter_context(nc.Block())

        def over_taps(engine, pair, do, after_head=None):
            def at_tap(j, i):
                for b in range(2):
                    do(2 * (pair * W + j) + b, 2 * pair + b, j if type(i) is int else i * STEP + j, i)

            for j in range(HEAD):
                at_tap(j, 0)
            if after_head is not None:
                after_head()
            with engine.Fori(0, (W - HEAD - TAIL) // STEP) as i:
                for j in range(HEAD, HEAD + STEP):
                    at_tap(j, i)
            for j in range(W - TAIL, W):
                at_tap(j, 0)

        def w_in_source(s):
            kind, layer, which, _ = STAGES[s]
            if kind == "ffn":
                return ffn_w_in[layer, which].rearrange("(k p) n -> p k n", p=P), F
            if kind == "conv":
                return conv_w_in[0].rearrange("(k p) n -> p k n", p=P), D
            return attn_w_qkv[0].rearrange("(k p) n -> p k n", p=P), None

        def w_out_source(s):
            kind, layer, which, _ = STAGES[s]
            w = {"ffn": ffn_w_out[layer, which], "conv": conv_w_out[0], "attn": attn_w_out[0]}[kind]
            return w.rearrange("(k p) n -> p k n", p=P)

        @block.sync
        def _(sp):
            def slot_free(n, i):
                if n >= RAW:
                    sp.wait_ge(lo_done, 2 * (n - RAW + 1) + i * 2 * RING)

            def load_first(s, n, c, part, i=0):
                slot_free(n, i)
                src, apart = w_in_source(s)
                dst = raw[n % RAW][:].rearrange("p (k n) -> p k n", k=4)
                rows = slice(4 * part, 4 * part + 4)
                for g in range(2):
                    if apart is not None:
                        sp.dma_start(dst[:, :, g * CH:(g + 1) * CH],
                                     src[:, rows, bass.ds(c * CH + g * apart, CH)]).then_inc(raw_ready[n % RAW], 16)
                    else:
                        two = slice(4 * part + 2 * g, 4 * part + 2 * g + 2)
                        sp.dma_start(dst[:, 2 * g:2 * g + 2, :],
                                     src[:, two, bass.ds(QK_CHUNKS[c] * BANK, BANK)]).then_inc(raw_ready[n % RAW], 16)

            def load_second(s, n, c, i=0):
                slot_free(n, i)
                src = w_out_source(s)
                dst = raw[n % RAW][:].rearrange("p (k n) -> p k n", k=2)
                for g in range(2):
                    sp.dma_start(dst[:, g:g + 1, :], src[:, bass.ds(c * 2 + g, 1), :]).then_inc(raw_ready[n % RAW], 16)

            for t in range(TT):
                sp.dma_start(xs[:, t, :], x[0, t * P:(t + 1) * P, :]).then_inc(x_loaded, 16)
            for s, (kind, _, _, chunks) in enumerate(STAGES):
                u = UNIT0[s]
                if kind == "ffn":
                    load_first(s, u, 0, 0)
                    load_first(s, u + 1, 0, 1)

                    def chunk(c, i):
                        n = u + 2 + 3 * (c - 1)
                        load_first(s, n, i * 2 + c, 0, i)
                        load_first(s, n + 1, i * 2 + c, 1, i)
                        load_second(s, n + 2, i * 2 + (c - 1), i)

                    chunk(1, 0)
                    chunk(2, 0)
                    with sp.Fori(0, (FCH - 3) // 2) as i:
                        chunk(3, i)
                        chunk(4, i)
                    load_second(s, u + 32, FCH - 1)
                else:
                    for c in range(chunks):
                        load_first(s, u + 2 * c, c, 0)
                        load_first(s, u + 2 * c + 1, c, 1)
                    for c in range(KT // 2):
                        load_second(s, u + 2 * chunks + c, c)
            for half in range(2):
                for t in range(TT):
                    sp.wait_ge(x_ready, 4 * 5 + 2 * half + t + 1)
                    sp.dma_start(out[0, t * P:(t + 1) * P, half * BANK:(half + 1) * BANK],
                                 xs[:, t, half * BANK:(half + 1) * BANK]).then_inc(out_stored, 16)
            sp.wait_ge(out_stored, 16 * 4)

        @block.gpsimd
        def _(pool):
            gains = [ffn_norm[0, 0], mix_norm[0], ffn_norm[0, 1], ffn_norm[1, 0], mix_norm[1], ffn_norm[1, 1]]
            def load_gain(n):
                pool.dma_start(gain[:, n % 2, :], gains[n].partition_broadcast(P)).then_inc(gain_loaded[n % 2], 16)

            load_gain(1)
            pool.dma_start(rows[0:W, :], conv_dw[0]).then_inc(rows_loaded, 16)
            for a, v in enumerate((conv_dw_b, conv_ln_g, conv_ln_b)):
                pool.dma_start(rows[W + a:W + a + 1, :], v).then_inc(rows_loaded, 16)
            pool.dma_start(b_out, conv_b_out[0].partition_broadcast(P)).then_inc(b_out_loaded, 16)
            nc.gpsimd.memset(up[:, :, 0:PAD], 0.0).then_inc(pad_zero, 1)
            nc.gpsimd.memset(exponent[:, :], -0.5).then_inc(exponent_set, 1)
            pool.wait_ge(exponent_set, 1)
            for n, (kind, a, t) in enumerate(POWERS):
                src, dst = {"turn": lambda: (msq[:, a, :], rstd[:, a, :]), "ln": lambda: (ln_v, ln_r),
                            "qk": lambda: (grp[:, t, :], grr[:, t, :]), "out": lambda: (grp[:, a, :], grr[:, a, :])}[kind]()
                pool.wait_ge(mean_done, n + 1)
                nc.gpsimd.tensor_tensor(dst, src, exponent[:, 0:src.shape[-1]], ALU.pow).then_inc(power_done, 1)
                if kind == "turn" and a < 4:
                    pool.wait_ge(xg_ready, 4 * (a + 1))
                    load_gain(a + 2)
                if kind == "turn" and a == CONV:
                    pool.wait_ge(turned, 4 * (CONV + 1))
                    pool.dma_start(b_in[:].rearrange("p t n -> p (t n)"),
                                   conv_b_in[0].partition_broadcast(P)).then_inc(bin_loaded, 16)
                    pool.wait_ge(tap_lo_set, 1)

                    def lower(d, k, tap, i):
                        if d >= DIAGS:
                            pool.wait_ge(diag_used, d - DIAGS + 1 + i * 2 * STEP)
                        nc.gpsimd.tensor_tensor(diag(1, d), ident,
                                                tap_lo[:, k, bass.ds(tap, 1)].to_broadcast([P, P]),
                                                ALU.mult).then_inc(diag_lo_set, 1)

                    pool.wait_ge(acc_done, 4 * CONV)
                    pool.wait_ge(pad_zero, 1)
                    for padded in (up_hi, up_lo):
                        nc.gpsimd.tensor_copy(padded[:, :, 0:PAD], up[:, 0:2, 0:PAD]).then_inc(pad_zero, 1)
                    for pair in range(PK // 2):
                        over_taps(pool, pair, lower)
                if kind == "turn" and a == CONV + 1:
                    pool.wait_ge(x_ready, 4 * (CONV + 1))
                    with nc.allow_non_contiguous_dma(reason="per-feature vectors, once"):
                        for c in range(2):
                            for b, v in enumerate((attn_q_norm, attn_k_norm)):
                                pool.dma_start(gq[c * DH:(c + 1) * DH, b:b + 1],
                                               v[0].rearrange("(d a) -> d a", a=1)).then_inc(at_loaded, 16)
                        pool.dma_start(gs, attn_subln_g[0].rearrange("(d a) -> d a", a=1)).then_inc(at_loaded, 16)
                    for b, v in enumerate((attn_lq1, attn_lk1, attn_lq2, attn_lk2)):
                        pool.dma_start(lam4[:, b, :], v[0].partition_broadcast(P)).then_inc(at_loaded, 16)

        @block.tensor
        def _(pe):
            def unit_ready(n, i=0):
                pe.wait_ge(lo_done, 2 * (n + 1) + i * 2 * RING)

            def products(dst, stat_hi, stat_lo, moves, first, last, begins, ends=None):
                for j, (m_hi, _) in enumerate(moves):
                    mm = pe.matmul(dst[j], stat_hi, m_hi, start=first, stop=False)
                    if begins and j == 0:
                        mm.then_inc(unit_begun, 1)
                for j, (_, m_lo) in enumerate(moves):
                    pe.matmul(dst[j], stat_hi, m_lo, start=False, stop=False)
                for j, (m_hi, _) in enumerate(moves):
                    mm = pe.matmul(dst[j], stat_lo, m_hi, start=False, stop=last)
                    if ends is not None:
                        mm.then_inc(ends, 1)

            def first_unit(n, part, banks, hooks=(), i=0):
                unit_ready(n, i)
                hi, lo = w_hi[n % RING], w_lo[n % RING]
                for k in range(4):
                    if k < len(hooks) and hooks[k] is not None:
                        hooks[k]()
                    kt = 4 * part + k
                    cols = slice(k * BANK, (k + 1) * BANK)
                    for t in range(TT):
                        tok = slice(t * P, (t + 1) * P)
                        end = kt == KT - 1
                        products([banks[t]], a_hi[:, kt, tok], a_lo[:, kt, tok], [(hi[:, cols], lo[:, cols])],
                                 kt == 0, end, k == 0 and t == 0, chunk_done if end else None)

            def second_unit(n, left, first, last, mid=None, i=0):
                unit_ready(n, i)
                hi, lo = w_hi[n % RING], w_lo[n % RING]

                def part(k, t, halves, end, begins):
                    s_hi, s_lo = left(k)
                    tok = slice(t * P, (t + 1) * P)
                    moves = [(hi[:, k * D + h * BANK:k * D + (h + 1) * BANK],
                              lo[:, k * D + h * BANK:k * D + (h + 1) * BANK]) for h in halves]
                    products([acc[:, 2 * t + h, :] for h in halves], s_hi[:, tok], s_lo[:, tok], moves,
                             first and k == 0, end, begins, acc_done if end else None)

                if last:
                    for h in range(2):
                        for t in range(TT):
                            for k in range(2):
                                part(k, t, (h,), k == 1, h == t == k == 0)
                else:
                    for k in range(2):
                        if k == 1 and mid is not None:
                            mid()
                        for t in range(TT):
                            part(k, t, (0, 1), False, t == k == 0)

            def turn(r, half):
                for t in range(TT):
                    pe.wait_ge(xg_ready, 4 * r + 2 * half + t + 1)
                    if half:
                        pe.wait_ge(a_lo_done, 4 * r + t + 1)
                    for k in range(4):
                        mm = pe.transpose(pt[:, t, k * P:(k + 1) * P],
                                          xg[:, t, half * BANK + k * P:half * BANK + (k + 1) * P], ident)
                    mm.then_inc(turned, 1)

            def a_ready(r, half):
                pe.wait_ge(a_lo_done, 4 * r + 2 * half + 2)

            def turn_rows():
                pe.wait_ge(rows_loaded, 16 * 4)
                for k in range(KT):
                    mm = pe.transpose(acc[:, 3, k * ROWS:(k + 1) * ROWS], rows[:, k * P:(k + 1) * P], ident[0:ROWS, 0:ROWS])
                mm.then_inc(rows_turned, 1)

            def ffn(s):
                f, u, c0 = FFN0[s], UNIT0[s], CHUNK0[s]
                banks = [pg[:, t, :] for t in range(TT)]
                banks0 = [acc[:, 2 * t, :] for t in range(TT)]

                def turn_hidden(c, i=0):
                    pe.wait_ge(chunk_out, 2 * (c0 + c + 1) + i * 4)
                    for k in range(2):
                        for t in range(TT):
                            mm = pe.transpose(pt[:, 0, (2 * k + t) * P:(2 * k + t + 1) * P],
                                              hid[:, t, k * P:(k + 1) * P], ident)
                    mm.then_inc(hid_turned, 1)

                def hidden_ready(c, i=0):
                    pe.wait_ge(h_lo_done, FCH * f + c + 1 + i * 2)

                def left(slot):
                    return lambda k: (h_hi[:, slot, k, :], h_lo[:, slot, k, :])

                turn(s, 0)
                a_ready(s, 0)
                first_unit(u, 0, banks0, (None, None, lambda: turn(s, 1)))
                a_ready(s, 1)
                first_unit(u + 1, 1, banks0, (turn_rows,) if s == 0 else ())

                def chunk(c, b, i, first):
                    if c > 1:
                        pe.wait_ge(chunk_out, 2 * (c0 + c) + i * 4)
                    n = u + 2 + 3 * (c - 1)
                    first_unit(n, 0, banks, (None, None, lambda: turn_hidden(c - 1, 0)) if first else (), i)
                    first_unit(n + 1, 1, banks, (), i)
                    hidden_ready(c - 1, i)
                    second_unit(n + 2, left((c - 1) % 2), first, False, lambda: turn_hidden(c, i), i)

                chunk(1, 1, 0, True)
                chunk(2, 0, 0, False)
                with pe.Fori(0, (FCH - 3) // 2) as i:
                    chunk(3, 1, i, False)
                    chunk(4, 0, i, False)
                hidden_ready(FCH - 1)
                second_unit(u + 32, left((FCH - 1) % 2), False, True)

            def a_left(w):
                return lambda k: (a_hi[:, 2 * w + k, :], a_lo[:, 2 * w + k, :])

            def conv(s):
                u, c0 = UNIT0[s], CHUNK0[s]
                chunks = STAGES[s][3]

                def turn_u(c):
                    pe.wait_ge(chunk_out, 2 * (c0 + c + 1))
                    if c >= 2:
                        pe.wait_ge(u_placed, c - 1)
                    for k in range(2):
                        for t in range(TT):
                            mm = pe.transpose(pt[:, c % 2, (2 * k + t) * P:(2 * k + t + 1) * P],
                                              hid[:, t, k * P:(k + 1) * P], ident)
                    mm.then_inc(u_turned, 1)

                turn(s, 0)
                a_ready(s, 0)
                for c in range(chunks):
                    banks = [(acc if c % 2 else pg)[:, t, :] for t in range(TT)]
                    if c >= 2:
                        pe.wait_ge(chunk_out, 2 * (c0 + c - 1))
                    mid = (lambda: turn(s, 1)) if c == 0 else (lambda: turn_u(c - 1))
                    first_unit(u + 2 * c, 0, banks, (None, None, mid))
                    if c == 0:
                        a_ready(s, 1)
                    first_unit(u + 2 * c + 1, 1, banks)
                for pair in range(PK // 2):
                    first = chunks - PK // 2 + pair
                    if pair:
                        pe.wait_ge(u_placed, first + 1)
                    pe.wait_ge(up_lo_set, pair + 1)
                    pe.wait_ge(pad_zero, 3)

                    def shifted(d, k, tap, i):
                        pe.wait_ge(diag_hi_set, d + 1 + i * 2 * STEP)
                        pe.wait_ge(diag_lo_set, d + 1 + i * 2 * STEP)
                        dst = acc[:, 2 - 2 * pair + k % 2, 0:T]
                        d_hi, d_lo = diag(0, d), diag(1, d)
                        u_hi, u_lo = up_hi[:, k % 2, bass.ds(tap, T)], up_lo[:, k % 2, bass.ds(tap, T)]
                        begins, ends = d % (2 * W) < 2, d % (2 * W) >= 2 * W - 2
                        pe.matmul(dst, d_hi, u_hi, start=begins, stop=False)
                        pe.matmul(dst, d_hi, u_lo, start=False, stop=False)
                        pe.matmul(dst, d_lo, u_hi, start=False, stop=ends).then_inc(diag_used, 1)

                    over_taps(pe, pair, shifted, (lambda: turn_u(chunks - 1)) if pair == 0 else None)
                for a, k0 in ((1, 4), (0, 0)):
                    for t, banks in enumerate((pg, pt)):
                        for k in range(k0, k0 + 4):
                            if t == 0 and k % 2 == 0:
                                if k < VK:
                                    pe.wait_ge(tap_done, W * (k + 2))
                                else:
                                    pe.wait_ge(cv_taken, k - VK + 2)
                            mm = pe.transpose(banks[:, a, (k % 4) * P:(k % 4 + 1) * P], cv[:, k, t * P:(t + 1) * P], ident)
                        mm.then_inc(c_turned, 1)
                for j in range(KT // 2):
                    for t in range(TT):
                        pe.wait_ge(ln_done[t], 1)
                        for k in range(2):
                            mm = pe.transpose((pg if j < 2 else pt)[:, j % 2, k * T + t * P:k * T + (t + 1) * P],
                                              xg[:, t, (2 * j + k) * P:(2 * j + k + 1) * P], ident)
                    mm.then_inc(n_turned, 1)
                for w in range(KT // 2):
                    pe.wait_ge(s_lo_done, w + 1)
                    second_unit(u + 2 * chunks + w, a_left(w), w == 0, w == KT // 2 - 1)

            def attn(s):
                u, c0 = UNIT0[s], CHUNK0[s]

                def turn_q(c):
                    for t in range(TT):
                        pe.wait_ge(qn_done, 2 * c + t + 1)
                        if c:
                            pe.wait_ge(q_placed, 2 * (c - 1) + t + 1)
                        for k in range(4):
                            mm = pe.transpose(pt[:, t, k * P:(k + 1) * P],
                                              xg[:, 0, t * BANK + k * P:t * BANK + (k + 1) * P], ident)
                        mm.then_inc(q_turned, 1)

                def scores(t, h):
                    n = t * H + h
                    keys = (t + 1) * P
                    if n >= 1:
                        pe.wait_ge(mx_done, n)
                    for c in range(2):
                        d = slice(c * DH, (c + 1) * DH)
                        mm = pe.matmul(acc[:, c, 0:keys], qT[d, h, t * P:(t + 1) * P], kT[d, h, 0:keys],
                                       start=True, stop=True)
                    mm.then_inc(sc_done, 1)

                def turn_p(t, h):
                    n = t * H + h
                    pe.wait_ge(pr_done, n + 1)
                    if n >= 2:
                        pe.wait_ge(p_placed, n - 1)
                    for b in range(t + 1):
                        mm = pe.transpose(pt[:, n % 2, b * P:(b + 1) * P], sc[:, n % 2, 0, b * P:(b + 1) * P], ident)
                    mm.then_inc(p_turned, 1)

                def values(t, h):
                    n = t * H + h
                    pe.wait_ge(p_placed, n + 1)
                    dst = pg[:, h // 4, (h % 4) * P:(h % 4 + 1) * P]
                    for b in range(t + 1):
                        left = aT[:, h, :] if t == 0 else aT[:, (n % 2) * 2 + b, :]
                        mm = pe.matmul(dst, left, vv[:, b, h * P:(h + 1) * P], start=b == 0, stop=b == t)
                    mm.then_inc(o_done, 1)

                turn(s, 0)
                a_ready(s, 0)
                for c in range(4):
                    banks = [(acc[:, 2 + t, :] if c % 2 else pg[:, t, :]) for t in range(TT)]
                    if c >= 2:
                        pe.wait_ge(chunk_out, 2 * (c0 + c - 1))
                    mid = (lambda: turn(s, 1)) if c == 0 else None
                    first_unit(u + 2 * c, 0, banks, (None, None, mid))
                    if c == 0:
                        a_ready(s, 1)
                    late = (lambda: turn_q(c - 1)) if c else None
                    first_unit(u + 2 * c + 1, 1, banks, (late,))
                for c in range(4, 6):
                    banks = [(acc[:, 2 + t, :] if c % 2 else pg[:, t, :]) for t in range(TT)]
                    pe.wait_ge(chunk_out, 2 * (c0 + c - 1))

                    def both(h):
                        if h == 0:
                            pe.wait_ge(q_placed, 8)
                        scores(0, h)
                        if h >= 1:
                            turn_p(0, h - 1)

                    if c == 4:
                        first_unit(u + 8, 0, banks, (None, None, lambda: turn_q(3)))
                        first_unit(u + 9, 1, banks, (None, lambda: both(0), None, lambda: both(1)))
                    else:
                        first_unit(u + 10, 0, banks, (None, lambda: both(2), None, lambda: both(3)))
                        first_unit(u + 11, 1, banks, (None, lambda: both(4), None, lambda: both(5)))
                both(6)
                both(7)
                scores(1, 0)
                turn_p(0, 7)
                pe.wait_ge(chunk_out, 2 * (c0 + 6))
                for h in range(H):
                    values(0, h)
                for h in range(1, H + 2):
                    if h < H:
                        scores(1, h)
                    if h <= H:
                        turn_p(1, h - 1)
                    if h >= 2:
                        if h == 2:
                            pe.wait_ge(on_done, 1)
                        values(1, h - 2)
                for t in range(TT):
                    for j in range(2):
                        pe.wait_ge(on_done, t + 1)
                        if t == 0:
                            pe.wait_ge(p_placed, 2 * H)
                        else:
                            pe.wait_ge(o_lo_done, j + 1)
                        for k in range(4):
                            mm = pe.transpose(pt[:, j, k * P:(k + 1) * P],
                                              xg[:, t, (4 * j + k) * P:(4 * j + k + 1) * P], ident)
                        mm.then_inc(on_turned, 1)
                for w in range(KT // 2):
                    pe.wait_ge(o_lo_done, 3 + w // 2)
                    second_unit(u + 12 + w, a_left(w), w == 0, w == KT // 2 - 1)

            pe.wait_ge(consts_loaded, 16)
            for s, (kind, _, _, _) in enumerate(STAGES):
                {"ffn": ffn, "conv": conv, "attn": attn}[kind](s)

        @block.scalar
        def _(act):
            def round_half(n, half, i=0):
                if half == 0:
                    act.wait_ge(raw_ready[n % RAW], 32 * (n // RAW + 1) + i * (32 * RING // RAW))
                    if n >= RING:
                        act.wait_ge(unit_begun, n - RING + 2 + i * RING)
                cols = slice(half * HALF, (half + 1) * HALF)
                nc.scalar.copy(w_hi[n % RING][:, cols], raw[n % RAW][:, cols]).then_inc(hi_done, 1)

            def tick(n, i=0, mid=None):
                if n + AHEAD < UNITS:
                    round_half(n + AHEAD, 0, i)
                if mid is not None:
                    mid()
                if n + AHEAD < UNITS:
                    round_half(n + AHEAD, 1, i)

            def turn(r, half):
                for t in range(TT):
                    act.wait_ge(turned, 4 * r + 2 * half + t + 1)
                    nc.scalar.copy(a_hi[:, 4 * half:4 * half + 4, t * P:(t + 1) * P],
                                   pt[:, t, :].rearrange("p (k n) -> p k n", k=4)).then_inc(a_hi_done, 1)
                for t in range(TT):
                    if r == 0:
                        act.wait_ge(x_loaded, 32)
                    else:
                        act.wait_ge(x_ready, 4 * (r - 1) + 2 * half + t + 1)
                    if 4 * r + 2 * half + t >= 2:
                        act.wait_ge(ss_done, 4 * r + 2 * half + t - 1)
                    nc.scalar.activation(junk[:, t, :], xs[:, t, half * BANK:(half + 1) * BANK], ACT.Square,
                                         accum_out=ss[:, r, t, half:half + 1]).then_inc(ss_done, 1)

            def ffn(s):
                f, u, c0 = FFN0[s], UNIT0[s], CHUNK0[s]

                def gate(c, i=0):
                    for t in range(TT):
                        act.wait_ge(chunk_done, 2 * (c0 + c) + t + 1 + i * 4)
                        src = pg[:, t, 0:CH] if c else acc[:, 2 * t, 0:CH]
                        nc.scalar.activation(sil[:, t, :], src, ACT.Silu,
                                             scale=rstd[:, s, t:t + 1]).then_inc(silu_done, 1)

                def hidden(c, i=0):
                    act.wait_ge(hid_turned, FCH * f + c + 1 + i * 2)
                    nc.scalar.copy(h_hi[:, c % 2, :, :].rearrange("p k n -> p (k n)"), pt[:, 0, :]).then_inc(h_hi_done, 1)

                if s == 0:
                    round_half(0, 0)
                    round_half(0, 1)
                    turn(s, 0)
                    round_half(1, 0)
                    round_half(1, 1)
                    turn(s, 1)
                    for n in range(2, AHEAD):
                        round_half(n, 0)
                        round_half(n, 1)
                    tick(u)
                    act.wait_ge(rows_turned, 1)
                    nc.scalar.copy(chan[:].rearrange("p k w -> p (k w)"), acc[:, 3, 0:KT * ROWS]).then_inc(chan_set, 1)
                    act.wait_ge(chan_set, 1)
                    nc.scalar.copy(tap_hi, chan[:, VK:KT, 0:W]).then_inc(chan_set, 1)
                else:
                    turn(s, 0)
                    tick(u)
                    turn(s, 1)
                tick(u + 1)
                act.wait_ge(power_done, POWER_AT["turn", s, 0] + 1)
                gate(0)
                tick(u + 2, 0, lambda: hidden(0))

                def chunk(c, i, skip_first):
                    n = u + 2 + 3 * (c - 1)
                    if not skip_first:
                        tick(n, i)
                    tick(n + 1, i)
                    gate(c, i)
                    tick(n + 2, i, lambda: hidden(c, i))

                chunk(1, 0, True)
                chunk(2, 0, False)
                peel = s == len(STAGES) - 1
                with act.Fori(0, (FCH - 3) // 2 - peel) as i:
                    chunk(3, i, False)
                    chunk(4, i, False)
                if peel:
                    chunk(FCH - 2, 0, False)
                    chunk(FCH - 1, 0, False)
                tick(u + 32)

            def conv(s):
                u, c0 = UNIT0[s], CHUNK0[s]
                chunks = STAGES[s][3]

                def place(c):
                    act.wait_ge(u_turned, c + 1)
                    dst = up[:, 2 * c:2 * c + 2, :] if 2 * c < VK else up_hi
                    if 2 * c > VK:
                        act.wait_ge(diag_used, W * (2 * c - VK))
                    nc.scalar.copy(dst[:, :, PAD:PAD + T],
                                   pt[:, c % 2, :].rearrange("p (k n) -> p k n", k=2)).then_inc(u_placed, 1)

                def upper(d, k, tap, i):
                    if d >= DIAGS:
                        act.wait_ge(diag_used, d - DIAGS + 1 + i * 2 * STEP)
                    nc.scalar.activation(diag(0, d), ident, ACT.Copy,
                                         scale=tap_hi[:, k, bass.ds(tap, 1)].bitcast(F32)).then_inc(diag_hi_set, 1)

                def take(pair):
                    act.wait_ge(diag_used, 2 * W * (pair + 1))
                    for b in range(2):
                        k = VK + 2 * pair + b
                        nc.scalar.activation(cv[:, k, :], acc[:, 2 - 2 * pair + b, 0:T], ACT.Identity,
                                             bias=chan[:, k, W:W + 1]).then_inc(cv_taken, 1)

                turn(s, 0)
                tick(u)
                turn(s, 1)
                for c in range(chunks):
                    if c:
                        tick(u + 2 * c, 0, lambda: place(c - 1))
                    tick(u + 2 * c + 1)
                    for t in range(TT):
                        act.wait_ge(ab_done, 2 * c + t + 1)
                        nc.scalar.activation(sg[:, t, :], ab[:, t, CH:2 * CH], ACT.Sigmoid).then_inc(sig_done, 1)
                over_taps(act, 0, upper)
                place(chunks - 1)
                over_taps(act, 1, upper, lambda: take(0))
                take(1)
                nc.scalar.activation(warm, chan[:, 0, 0:1], ACT.Silu)
                act.wait_ge(power_done, POWER_AT["ln", 0, 0] + 1)
                act.wait_ge(ln_b_set, 1)
                nc.scalar.activation(xg[:, 1, :], pt[:, :, :].rearrange("p a n -> p (a n)"), ACT.Identity,
                                     bias=ln_b, scale=ln_r[:, 1:2]).then_inc(ln_done[1], 1)
                for j in range(KT // 2):
                    act.wait_ge(n_turned, j + 1)
                    for k in range(2):
                        kt = 2 * j + k
                        mm = nc.scalar.activation(cv[:, kt, :], (pg if j < 2 else pt)[:, j % 2, k * T:(k + 1) * T], ACT.Silu,
                                                  bias=chan[:, kt, W + 2:W + 3], scale=chan[:, kt, W + 1:W + 2])
                    mm.then_inc(act_done, 1)
                    act.wait_ge(act_done, j + 1)
                    nc.scalar.copy(a_hi[:, 2 * j:2 * j + 2, :], cv[:, 2 * j:2 * j + 2, :]).then_inc(s_hi_done, 1)
                tick(u + 2 * chunks)
                for w in range(1, 4):
                    tick(u + 2 * chunks + w)

            def attn(s):
                u, c0 = UNIT0[s], CHUNK0[s]

                def squares(c):
                    for t in range(TT):
                        act.wait_ge(chunk_out, 2 * (c0 + c) + t + 1)
                        nc.scalar.activation(xg[:, 1, t * BANK:(t + 1) * BANK], vv[:, t, 0:BANK],
                                             ACT.Square).then_inc(sq_done, 1)

                def place_q(c):
                    dst, a = (qT, 0) if c % 2 == 0 else (kT, 1)
                    if c == 0:
                        act.wait_ge(at_loaded, 16 * 9)
                    for t in range(TT):
                        act.wait_ge(q_turned, 2 * c + t + 1)
                        nc.scalar.activation(dst[:, 4 * (c // 2):4 * (c // 2) + 4, t * P:(t + 1) * P],
                                             pt[:, t, :].rearrange("p (k n) -> p k n", k=4), ACT.Copy,
                                             scale=gq[:, a:a + 1]).then_inc(q_placed, 1)

                def exps(n):
                    keys = (n // H + 1) * P
                    act.wait_ge(mx_done, n + 1)
                    for c in range(2):
                        mm = nc.scalar.activation(sc[:, n % 2, c, 0:keys], sc[:, n % 2, c, 0:keys], ACT.Exp,
                                                  bias=mx[:, n % 2, c:c + 1], accum_out=sm[:, n % 2, c:c + 1])
                    mm.then_inc(ex_done, 1)

                def place_p(n):
                    t, h = divmod(n, H)
                    act.wait_ge(p_turned, n + 1)
                    if t == 0:
                        nc.scalar.copy(aT[:, h, :], pt[:, n % 2, 0:P]).then_inc(p_placed, 1)
                    else:
                        act.wait_ge(o_done, H if h < 2 else H + h - 1)
                        b = (n % 2) * 2
                        nc.scalar.copy(aT[:, b:b + 2, :], pt[:, n % 2, 0:2 * P].rearrange("p (b n) -> p b n", b=2)).then_inc(p_placed, 1)

                turn(s, 0)
                tick(u)
                turn(s, 1)
                tick(u + 1)
                act.wait_ge(lam_sum, 1)
                nc.scalar.activation(lsum, lsum, ACT.Exp).then_inc(lam_exp, 1)
                squares(0)
                for c in range(1, 4):
                    tick(u + 2 * c)
                    tick(u + 2 * c + 1, 0, lambda: place_q(c - 1))
                    squares(c)
                tick(u + 8, 0, lambda: place_q(3))
                tick(u + 9)
                for n in range(H):
                    exps(n)
                    if n >= 1:
                        place_p(n - 1)
                    if n in (2, 4):
                        tick(u + 10 + (n == 4))
                exps(H)
                place_p(H - 1)
                for n in range(H + 1, 2 * H):
                    exps(n)
                    if n == H + 2:
                        act.wait_ge(o_done, H)
                        nc.scalar.activation(xg[:, 1, :], pg[:, :, :].rearrange("p a n -> p (a n)"), ACT.Square).then_inc(osq_done, 1)
                    place_p(n - 1)
                place_p(2 * H - 1)
                act.wait_ge(o_done, 2 * H)
                act.wait_ge(on_done, 1)
                nc.scalar.activation(xg[:, 1, :], pg[:, :, :].rearrange("p a n -> p (a n)"), ACT.Square).then_inc(osq_done, 1)
                tick(u + 12)
                for t in range(TT):
                    for j in range(2):
                        act.wait_ge(on_turned, 2 * t + j + 1)
                        nc.scalar.activation(a_hi[:, 4 * j:4 * j + 4, t * P:(t + 1) * P],
                                             pt[:, j, :].rearrange("p (k n) -> p k n", k=4), ACT.Copy,
                                             scale=gs).then_inc(o_hi_done, 1)
                for w in range(1, 4):
                    tick(u + 12 + w)

            act.dma_start(gain[:, 0, :], ffn_norm[0, 0].partition_broadcast(P)).then_inc(gain0_loaded, 16)
            act.dma_start(consts[:, :], shape_consts).then_inc(consts_loaded, 16)
            for s, (kind, _, _, _) in enumerate(STAGES):
                {"ffn": ffn, "conv": conv, "attn": attn}[kind](s)

        @block.vector
        def _(dve):
            links = [0]

            def link(ins):
                links[0] += 1
                ins.then_inc(step, 1)
                dve.wait_ge(step, links[0])

            def power_ready(*key):
                dve.wait_ge(power_done, POWER_AT[key] + 1)

            def rest_half(n, half, i=0):
                dve.wait_ge(hi_done, 2 * n + half + 1 + i * 2 * RING)
                cols = slice(half * HALF, (half + 1) * HALF)
                nc.vector.tensor_tensor(w_lo[n % RING][:, cols], raw[n % RAW][:, cols],
                                        w_hi[n % RING][:, cols].bitcast(F32), ALU.subtract).then_inc(lo_done, 1)

            def tick(n, i=0, mid=None):
                if n + AHEAD < UNITS:
                    rest_half(n + AHEAD, 0, i)
                if mid is not None:
                    mid()
                if n + AHEAD < UNITS:
                    rest_half(n + AHEAD, 1, i)

            def update(r, half, scale):
                cols = slice(half * BANK, (half + 1) * BANK)
                for t in range(TT):
                    if r:
                        dve.wait_ge(acc_done, 4 * (r - 1) + 2 * half + t + 1)
                        nc.vector.scalar_tensor_tensor(out=xs[:, t, cols], in0=acc[:, 2 * t + half, :], scalar=scale,
                                                       in1=xs[:, t, cols], op0=ALU.mult, op1=ALU.add).then_inc(x_ready, 1)
                    if r < len(STAGES):
                        if r:
                            dve.wait_ge(x_ready, 4 * (r - 1) + 2 * half + t + 1)
                        else:
                            dve.wait_ge(x_loaded, 32)
                        if r:
                            dve.wait_ge(gain_loaded[r % 2], 16 * ((r + 1) // 2))
                        else:
                            dve.wait_ge(gain0_loaded, 16)
                        nc.vector.tensor_tensor(xg[:, t, cols], xs[:, t, cols], gain[:, r % 2, cols],
                                                ALU.mult).then_inc(xg_ready, 1)

            def turn_rest(r, half):
                for t in range(TT):
                    dve.wait_ge(a_hi_done, 4 * r + 2 * half + t + 1)
                    dst = (slice(None), slice(4 * half, 4 * half + 4), slice(t * P, (t + 1) * P))
                    nc.vector.tensor_tensor(a_lo[dst], pt[:, t, :].rearrange("p (k n) -> p k n", k=4),
                                            a_hi[dst].bitcast(F32), ALU.subtract).then_inc(a_lo_done, 1)

            def token_factors(r):
                dve.wait_ge(ss_done, 4 * (r + 1))
                link(nc.vector.tensor_tensor(msq[:, r, :], ss[:, r, :, 0], ss[:, r, :, 1], ALU.add))
                nc.vector.tensor_scalar(msq[:, r, :], msq[:, r, :], 1.0 / D, EPS, ALU.mult, ALU.add).then_inc(mean_done, 1)

            def enter(s, scale):
                update(s, 0, scale)
                if s == 0:
                    update(s, 1, scale)
                    rest_half(0, 0)
                    rest_half(0, 1)
                    turn_rest(s, 0)
                    rest_half(1, 0)
                    rest_half(1, 1)
                    turn_rest(s, 1)
                    token_factors(s)
                    for n in range(2, AHEAD):
                        rest_half(n, 0)
                        rest_half(n, 1)
                    tick(UNIT0[s])
                    dve.wait_ge(chan_set, 2)
                    nc.vector.tensor_tensor(tap_lo, chan[:, VK:KT, 0:W], tap_hi.bitcast(F32), ALU.subtract).then_inc(tap_lo_set, 1)
                    return
                turn_rest(s, 0)
                tick(UNIT0[s])
                update(s, 1, scale)
                turn_rest(s, 1)
                token_factors(s)

            def ffn(s):
                f, u, c0 = FFN0[s], UNIT0[s], CHUNK0[s]

                def gated(c, i=0):
                    for t in range(TT):
                        dve.wait_ge(silu_done, 2 * (FCH * f + c) + t + 1 + i * 4)
                        src = pg[:, t, CH:2 * CH] if c else acc[:, 2 * t, CH:2 * CH]
                        nc.vector.scalar_tensor_tensor(out=hid[:, t, :], in0=src,
                                                       scalar=rstd[:, s, t:t + 1], in1=sil[:, t, :],
                                                       op0=ALU.mult, op1=ALU.mult).then_inc(chunk_out, 1)

                def hidden(c, i=0):
                    dve.wait_ge(h_hi_done, FCH * f + c + 1 + i * 2)
                    nc.vector.tensor_tensor(h_lo[:, c % 2, :, :].rearrange("p k n -> p (k n)"), pt[:, 0, :],
                                            h_hi[:, c % 2, :, :].rearrange("p k n -> p (k n)").bitcast(F32),
                                            ALU.subtract).then_inc(h_lo_done, 1)

                tick(u + 1)
                power_ready("turn", s, 0)
                gated(0)
                tick(u + 2, 0, lambda: hidden(0))

                def chunk(c, i, skip_first):
                    n = u + 2 + 3 * (c - 1)
                    if not skip_first:
                        tick(n, i)
                    tick(n + 1, i)
                    gated(c, i)
                    tick(n + 2, i, lambda: hidden(c, i))

                chunk(1, 0, True)
                chunk(2, 0, False)
                peel = s == len(STAGES) - 1
                with dve.Fori(0, (FCH - 3) // 2 - peel) as i:
                    chunk(3, i, False)
                    chunk(4, i, False)
                if peel:
                    chunk(FCH - 2, 0, False)
                    chunk(FCH - 1, 0, False)
                tick(u + 32)

            def conv(s):
                u, c0 = UNIT0[s], CHUNK0[s]
                chunks = STAGES[s][3]

                def glu(c):
                    src = acc if c % 2 else pg
                    for t in range(TT):
                        dve.wait_ge(chunk_done, 2 * (c0 + c) + t + 1)
                        nc.vector.scalar_tensor_tensor(
                            out=ab[:, t, :].rearrange("p (g n) -> p g n", g=2),
                            in0=src[:, t, :].rearrange("p (g n) -> p g n", g=2),
                            scalar=rstd[:, s, t:t + 1], in1=b_in[:, :, c * CH:(c + 1) * CH],
                            op0=ALU.mult, op1=ALU.add).then_inc(ab_done, 1)
                    for t in range(TT):
                        dve.wait_ge(sig_done, 2 * c + t + 1)
                        nc.vector.tensor_tensor(hid[:, t, :], ab[:, t, 0:CH], sg[:, t, :], ALU.mult).then_inc(chunk_out, 1)

                def first_tap(c):
                    dve.wait_ge(u_placed, c + 1)
                    for k in (2 * c, 2 * c + 1):
                        nc.vector.tensor_scalar(cv[:, k, :], up[:, k, 0:T], chan[:, k, 0:1], chan[:, k, W:W + 1],
                                                ALU.mult, ALU.add).then_inc(tap_done, 1)

                def more_taps(c, start, stop, step):
                    with dve.Fori(0, (stop - start) // step) as i:
                        for j in range(start, start + step):
                            for b, k in enumerate((2 * c, 2 * c + 1)):
                                dve.wait_ge(tap_done, 2 * (W * c + j - 1) + b + 1 + i * 2 * step)
                                nc.vector.scalar_tensor_tensor(
                                    out=cv[:, k, :], in0=up[:, k, bass.ds(i * step + j, T)],
                                    scalar=chan[:, k, bass.ds(i * step + j, 1)], in1=cv[:, k, :],
                                    op0=ALU.mult, op1=ALU.add).then_inc(tap_done, 1)

                def lower_input(c):
                    dve.wait_ge(u_placed, c + 1)
                    nc.vector.tensor_tensor(up_lo[:, :, PAD:PAD + T], pt[:, c % 2, :].rearrange("p (k n) -> p k n", k=2),
                                            up_hi[:, :, PAD:PAD + T].bitcast(F32), ALU.subtract).then_inc(up_lo_set, 1)

                dve.wait_ge(bin_loaded, 16)
                dve.wait_ge(pad_zero, 1)
                power_ready("turn", s, 0)
                tick(u + 1)
                glu(0)
                tick(u + 2)
                tick(u + 3)
                glu(1)
                first_tap(0)
                more_taps(0, 1, 5, 2)
                tick(u + 4)
                tick(u + 5)
                glu(2)
                more_taps(0, 5, 9, 2)
                tick(u + 6)
                lower_input(2)
                tick(u + 7)
                glu(3)
                more_taps(0, 9, W - 2, 5)
                more_taps(0, W - 2, W, 1)
                first_tap(1)
                more_taps(1, 1, 3, 1)
                lower_input(3)
                more_taps(1, 3, W, 7)
                for a in (1, 0):
                    for t, banks in enumerate((pg, pt)):
                        dve.wait_ge(c_turned, (2 - 2 * a) + t + 1)
                        mm = nc.vector.bn_stats(bn[:, t, a, :], banks[:, a, :])
                        if a == 0:
                            link(mm)
                            link(nc.vector.bn_aggr(mv[:, t, :], bn[:, t, :, :]))
                nc.vector.tensor_scalar(ln_v, mv[:, :, 1], EPS, None, ALU.add).then_inc(mean_done, 1)
                power_ready("ln", 0, 0)
                nc.vector.scalar_tensor_tensor(out=ln_b, in0=mv[:, 1, 0:1], scalar=-1.0, in1=ln_r[:, 1:2],
                                               op0=ALU.mult, op1=ALU.mult).then_inc(ln_b_set, 1)
                nc.vector.tensor_scalar(xg[:, 0, :], pg[:, :, :].rearrange("p a n -> p (a n)"),
                                        mv[:, 0, 0:1], ln_r[:, 0:1], ALU.subtract, ALU.mult).then_inc(ln_done[0], 1)
                for j in range(KT // 2):
                    dve.wait_ge(s_hi_done, j + 1)
                    nc.vector.tensor_tensor(a_lo[:, 2 * j:2 * j + 2, :], cv[:, 2 * j:2 * j + 2, :],
                                            a_hi[:, 2 * j:2 * j + 2, :].bitcast(F32), ALU.subtract).then_inc(s_lo_done, 1)
                dve.wait_ge(b_out_loaded, 16)
                tick(u + 2 * chunks)
                for t in range(TT):
                    mm = nc.vector.tensor_tensor(xs[:, t, :], xs[:, t, :], b_out, ALU.add)
                link(mm)
                for w in range(1, 4):
                    tick(u + 2 * chunks + w)

            def attn(s):
                u, c0 = UNIT0[s], CHUNK0[s]

                def lambdas():
                    dve.wait_ge(at_loaded, 16 * 9)
                    for a in range(2):
                        link(nc.vector.tensor_tensor(lprod, lam4[:, 2 * a, :], lam4[:, 2 * a + 1, :], ALU.mult))
                        mm = nc.vector.reduce_sum(lsum[:, a:a + 1], lprod, AX_X)
                        if a == 0:
                            link(mm)
                    mm.then_inc(lam_sum, 1)

                def take(c):
                    src = [(acc[:, 2 + t, :] if c % 2 else pg[:, t, :]) for t in range(TT)]
                    for t in range(TT):
                        dve.wait_ge(chunk_done, 2 * (c0 + c) + t + 1)
                        cols = slice(0, BANK) if c < 4 else slice((c - 4) * BANK, (c - 3) * BANK)
                        nc.vector.tensor_scalar(vv[:, t, cols], src[t], rstd[:, s, t:t + 1], None,
                                                ALU.mult).then_inc(chunk_out, 1)

                def norm_qk(c):
                    under = float(DH) if c % 2 == 0 else 1.0
                    for t in range(TT):
                        dve.wait_ge(sq_done, 2 * c + t + 1)
                        link(nc.vector.reduce_sum(grp[:, t, :], xg[:, 1, t * BANK:(t + 1) * BANK].rearrange("p (g d) -> p g d", d=DH), AX_X))
                        nc.vector.tensor_scalar(grp[:, t, :], grp[:, t, :], under / DH, under * EPS,
                                                ALU.mult, ALU.add).then_inc(mean_done, 1)
                        power_ready("qk", c, t)
                        if c:
                            dve.wait_ge(q_turned, 2 * (c - 1) + t + 1)
                        nc.vector.tensor_tensor(xg[:, 0, t * BANK:(t + 1) * BANK].rearrange("p (g d) -> p g d", d=DH),
                                                vv[:, t, 0:BANK].rearrange("p (g d) -> p g d", d=DH),
                                                grr[:, t, :].rearrange("p (g a) -> p g a", a=1).to_broadcast([P, BANK // DH, DH]),
                                                ALU.mult).then_inc(qn_done, 1)

                def biased(n):
                    t, h = divmod(n, H)
                    keys = (t + 1) * P
                    slope = 2.0 ** (-8.0 * (h + 1) / H)
                    dve.wait_ge(sc_done, n + 1)
                    if n >= 2:
                        dve.wait_ge(p_turned, n - 1)
                    d = dist[:, 2 * P - keys:2 * P].rearrange("p (a n) -> p a n", a=1).to_broadcast([P, 2, keys])
                    link(nc.vector.scalar_tensor_tensor(out=sc[:, n % 2, :, 0:keys], in0=d, scalar=-slope,
                                                        in1=acc[:, 0:2, 0:keys], op0=ALU.mult, op1=ALU.add))
                    link(nc.vector.reduce_max(mx[:, n % 2, :], sc[:, n % 2, :, 0:keys], AX_X))
                    nc.vector.tensor_scalar(mx[:, n % 2, :], mx[:, n % 2, :], -1.0, None, ALU.mult).then_inc(mx_done, 1)

                def combined(n):
                    keys = (n // H + 1) * P
                    dve.wait_ge(ex_done, n + 1)
                    link(nc.vector.reciprocal(rs[:, n % 2, :], sm[:, n % 2, :]))
                    link(nc.vector.tensor_tensor(rs[:, n % 2, 1:2], rs[:, n % 2, 1:2], nlam, ALU.mult))
                    link(nc.vector.tensor_scalar(sc[:, n % 2, 0, 0:keys], sc[:, n % 2, 0, 0:keys],
                                                 rs[:, n % 2, 0:1], None, ALU.mult))
                    nc.vector.scalar_tensor_tensor(out=sc[:, n % 2, 0, 0:keys], in0=sc[:, n % 2, 1, 0:keys],
                                                   scalar=rs[:, n % 2, 1:2], in1=sc[:, n % 2, 0, 0:keys],
                                                   op0=ALU.mult, op1=ALU.add).then_inc(pr_done, 1)

                def norm_out(t):
                    dve.wait_ge(osq_done, t + 1)
                    g = grp[:, t, :]
                    link(nc.vector.reduce_sum(g, xg[:, 1, :].rearrange("p (g d) -> p g d", g=H), AX_X))
                    under = (1.0 - LAMBDA_INIT) ** -2
                    nc.vector.tensor_scalar(g, g, under / (2 * DH), under * EPS, ALU.mult, ALU.add).then_inc(mean_done, 1)
                    power_ready("out", t, 0)
                    nc.vector.tensor_tensor(xg[:, t, :].rearrange("p (g d) -> p g d", g=H),
                                            pg[:, :, :].rearrange("p a (g d) -> p (a g) d", d=P),
                                            grr[:, t, :].rearrange("p (g a) -> p g a", a=1).to_broadcast([P, H, P]),
                                            ALU.mult).then_inc(on_done, 1)

                lambdas()
                tick(u + 1)
                power_ready("turn", s, 0)
                take(0)
                for c in range(1, 4):
                    norm_qk(c - 1)
                    tick(u + 2 * c)
                    tick(u + 2 * c + 1)
                    take(c)
                dve.wait_ge(lam_exp, 1)
                link(nc.vector.tensor_tensor(nlam, lsum[:, 1:2], lsum[:, 0:1], ALU.subtract))
                link(nc.vector.tensor_scalar(nlam, nlam, -LAMBDA_INIT, None, ALU.add))
                norm_qk(3)
                tick(u + 8)
                tick(u + 9)
                biased(0)
                for n in range(1, H):
                    biased(n)
                    combined(n - 1)
                    if n == 1:
                        take(4)
                    if n in (3, 5):
                        tick(u + 10 + (n == 5))
                take(5)
                biased(H)
                combined(H - 1)
                for n in range(H + 1, 2 * H):
                    biased(n)
                    combined(n - 1)
                    if n == H + 2:
                        norm_out(0)
                combined(2 * H - 1)
                norm_out(1)
                tick(u + 12)
                for t in range(TT):
                    for j in range(2):
                        dve.wait_ge(o_hi_done, 2 * t + j + 1)
                        dst = (slice(None), slice(4 * j, 4 * j + 4), slice(t * P, (t + 1) * P))
                        nc.vector.scalar_tensor_tensor(out=a_lo[dst], in0=pt[:, j, :].rearrange("p (k n) -> p k n", k=4),
                                                       scalar=gs, in1=a_hi[dst].bitcast(F32), op0=ALU.mult,
                                                       op1=ALU.subtract).then_inc(o_lo_done, 1)
                for w in range(1, 4):
                    tick(u + 12 + w)

            for s, (kind, _, _, _) in enumerate(STAGES):
                enter(s, 0.5 if s and STAGES[s - 1][0] == "ffn" else 1.0)
                {"ffn": ffn, "conv": conv, "attn": attn}[kind](s)
            update(len(STAGES), 0, 0.5)
            update(len(STAGES), 1, 0.5)


NAMES = ["x", "ffn_norm", "ffn_w_in", "ffn_w_out", "mix_norm", "conv_w_in", "conv_b_in", "conv_dw", "conv_dw_b",
         "conv_ln_g", "conv_ln_b", "conv_w_out", "conv_b_out", "attn_w_qkv", "attn_q_norm", "attn_k_norm",
         "attn_lq1", "attn_lk1", "attn_lq2", "attn_lk2", "attn_subln_g", "attn_w_out"]


def kernel(**inputs):
    import concourse.bacc as bacc
    from concourse.bass_utils import run_bass_kernel_spmd as run

    nc = bacc.Bacc("TRN2", target_bir_lowering=False, num_devices=1)
    arrays, args = {}, []
    for name in NAMES:
        a = np.ascontiguousarray(inputs[name])
        arrays[f"in_{name}"] = a
        args.append(nc.dram_tensor(f"in_{name}", a.shape, mybir.dt.from_np(a.dtype), kind="ExternalInput").ap())
    away = np.arange(P)[:, None] + P - np.arange(2 * P)[None, :]
    consts = np.concatenate([np.eye(P), np.where(away < 0, FAR, away)], axis=1).astype(np.float32)
    arrays["in_consts"] = consts
    args.append(nc.dram_tensor("in_consts", consts.shape, F32, kind="ExternalInput").ap())
    y = nc.dram_tensor("out_y", (1, T, D), F32, kind="ExternalOutput").ap()
    trunk(nc, *args, y)
    return run(nc, [arrays], core_ids=[0]).results[0]["out_y"]
```

```python
import math
from contextlib import ExitStack

import numpy as np
import concourse.bass as bass
from concourse import mybir

ALU = mybir.AluOpType
ACT = mybir.ActivationFunctionType
F32 = mybir.dt.float32
F32R = mybir.dt.float32r
AX_X = mybir.AxisListType.X

P = 128
D = 1024
T = 256
TT = T // P
KT = D // P
F = 2816
W = 31
PAD = W - 1
H = 8
DH = 64
EPS = 1e-6
DEPTH = 2
LAMBDA_INIT = 0.8 - 0.6 * math.exp(-0.3 * 1)
HUGE = 3e38
FAR = 1e36

CH = 256
FCH = F // CH
BANK = 512
UNIT = 2048
HALF = UNIT // 2
RAW = 3
RING = 6
AHEAD = 4
MIX = 7600
VK = 4
PK = KT - VK
SLOTS = 3
DIAGS = 2 * SLOTS
ROWS = W + 3
HEAD, STEP, TAIL = 3, 2 * SLOTS, 4

STAGES = [("ffn", 0, 0, FCH), ("conv", 0, 0, 2 * D // BANK), ("ffn", 0, 1, FCH),
          ("ffn", 1, 0, FCH), ("attn", 1, 0, 3 * D // BANK), ("ffn", 1, 1, FCH)]
SECOND = {"ffn": FCH, "conv": KT // 2, "attn": KT // 2}
UNIT0, CHUNK0, OUT0, FFN0 = [], [], [], []
_u = _c = _o = _f = 0
for _kind, _, _, _chunks in STAGES:
    UNIT0.append(_u)
    CHUNK0.append(_c)
    OUT0.append(_o)
    FFN0.append(_f)
    _u += 2 * _chunks + SECOND[_kind]
    _c += _chunks
    _o += _chunks if _kind != "attn" else 0
    _f += _kind == "ffn"
UNITS = _u
CONV, ATTN = 1, 4
POWERS = [("turn", 0, 0), ("turn", 1, 0), ("ln", 0, 0), ("turn", 2, 0), ("turn", 3, 0), ("turn", 4, 0)] \
    + [("qk", m, t) for m in range(4) for t in range(TT)] \
    + [("out", g, t) for g in range(2) for t in range(TT)] + [("turn", 5, 0)]
POWER_AT = {key: n for n, key in enumerate(POWERS)}
GROUP = 4
QKV_CHUNKS = [0, 2, 4, 1, 3, 5]
Q_OR_K = [0, 1, 3, 4]
STEPS = H * TT


def trunk(nc, x, ffn_norm, ffn_w_in, ffn_w_out, mix_norm, conv_w_in, conv_b_in, conv_dw, conv_dw_b,
          conv_ln_g, conv_ln_b, conv_w_out, conv_b_out, attn_w_qkv, attn_q_norm, attn_k_norm,
          attn_lq1, attn_lk1, attn_lq2, attn_lk2, attn_subln_g, attn_w_out, shape_consts, out):
    with ExitStack() as ctx:
        def sb(name, shape, dt=F32):
            return ctx.enter_context(nc.sbuf_tensor(name, shape, dt))

        def sem(name):
            return ctx.enter_context(nc.semaphore(name))

        raw = [sb(f"raw{i}", [P, UNIT]) for i in range(RAW)]
        w_hi = [sb(f"w_hi{i}", [P, UNIT], F32R) for i in range(RING)]
        w_lo = [sb(f"w_lo{i}", [P, UNIT], F32R) for i in range(RING)]
        xs = sb("xs", [P, TT, D])
        xg = sb("xg", [P, TT, D])
        gain = sb("gain", [P, 2, D])
        a_hi = sb("a_hi", [P, KT, T], F32R)
        a_lo = sb("a_lo", [P, KT, T], F32R)
        h_hi = sb("h_hi", [P, 2, 2, T], F32R)
        h_lo = sb("h_lo", [P, 2, 2, T], F32R)
        hs = sb("hs", [P, 2, TT, CH])
        hid, sil = hs[:, 0, :, :], hs[:, 1, :, :]
        consts = sb("consts", [P, P + 2 * P])
        ident = consts[:, 0:P]
        dist = consts[:, P:3 * P]
        ss = sb("ss", [P, 6, TT, 2])
        rstd = sb("rstd", [P, 6, TT])
        msq = sb("msq", [P, 6, TT])
        exponent = sb("exponent", [P, 8])
        more_diags = sb("more_diags", [P, 2, DIAGS - 3, P], F32R)
        mix = sb("mix", [P, MIX])

        junk = mix[:, 0:2 * BANK].rearrange("p (t n) -> p t n", t=TT)

        acc = ctx.enter_context(nc.psum_tensor("acc", [P, 4, BANK], F32))
        pg = ctx.enter_context(nc.psum_tensor("pg", [P, 2, BANK], F32))
        pt = ctx.enter_context(nc.psum_tensor("pt", [P, 2, BANK], F32))

        at = 0
        ab = mix[:, at:at + TT * BANK].rearrange("p (t n) -> p t n", t=TT)
        at += TT * BANK
        sg = sil
        up = mix[:, at:at + VK * (PAD + T)].rearrange("p (k n) -> p k n", k=VK)
        at += VK * (PAD + T)
        cv = mix[:, at:at + KT * T].rearrange("p (k n) -> p k n", k=KT)
        at += KT * T
        rows = cv[:].rearrange("p k n -> p (k n)")[0:ROWS, 0:D]
        chan = mix[:, at:at + KT * ROWS].rearrange("p (k w) -> p k w", k=KT)
        at += KT * ROWS
        tap_hi = mix[:, at:at + PK * W].rearrange("p (k w) -> p k w", k=PK).bitcast(F32R)
        at += PK * W
        tap_lo = mix[:, at:at + PK * W].rearrange("p (k w) -> p k w", k=PK)
        at += PK * W
        b_out = mix[:, at:at + D]
        at += D
        bn = mix[:, at:at + 24].rearrange("p (t a s) -> p t a s", t=TT, a=2)
        at += 24
        mv = mix[:, at:at + 4].rearrange("p (t a) -> p t a", t=TT)
        at += 4
        ln_v, ln_r, ln_b = mix[:, at:at + 2], mix[:, at + 2:at + 4], mix[:, at + 4:at + 5]
        at += 5
        warm = mix[:, at:at + 1]
        at += 1
        in_h = [h[:].rearrange("p a k n -> p (a k n)") for h in (h_hi, h_lo)]
        up_hi, up_lo = (h[:, 0:2 * (PAD + T)].rearrange("p (k n) -> p k n", k=2) for h in in_h)

        def diag(part, d):
            slot, here = d % DIAGS, 3
            first = 2 * (PAD + T) + slot * P
            return in_h[part][:, first:first + P] if slot < here else more_diags[:, part, slot - here, :]

        assert at <= MIX
        b_in = xg
        at = 0
        qT = mix[:, at:at + H * T].rearrange("p (h n) -> p h n", h=H)
        at += H * T
        kT = mix[:, at:at + H * T].rearrange("p (h n) -> p h n", h=H)
        at += H * T
        vv = mix[:, at:at + TT * D].rearrange("p (t n) -> p t n", t=TT)
        at += TT * D
        sc = mix[:, at:at + 2 * 2 * T].rearrange("p (s c n) -> p s c n", s=2, c=2)
        at += 2 * 2 * T
        aT = hs[:, 0, :, :].rearrange("p t (b n) -> p t b n", n=P)
        bias = hs[:, 1, :, :]
        o_sb = gain[:, 0, :].rearrange("p (t n) -> p t n", t=TT)
        small = mix[:, at:at + 400]
        at += 400
        assert at <= MIX
        gq = small[:, 0:2]
        gs = small[:, 2:3]
        lam4 = small[:, 4:4 + 4 * DH].rearrange("p (a d) -> p a d", a=4)
        lsum = small[:, 260:262]
        nlam = small[:, 262:263]
        grp = small[:, 264:280].rearrange("p (t g) -> p t g", t=TT)
        grr = small[:, 364:380].rearrange("p (t g) -> p t g", t=TT)
        mx = small[:, 280:284].rearrange("p (s c) -> p s c", s=2)
        sm = small[:, 284:288].rearrange("p (s c) -> p s c", s=2)
        rs = small[:, 288:296].rearrange("p (s c) -> p s c", s=4)
        fac = small[:, 296:298]
        lprod = small[:, 300:364]

        def score_banks(n):
            return acc if n < GROUP * TT else pg

        raw_ready = [sem(f"raw_ready{i}") for i in range(RAW)]
        hi_done = sem("hi_done")
        lo_done = sem("lo_done")
        unit_begun = sem("unit_begun")
        x_loaded = [sem(f"x_loaded{t}") for t in range(TT)]
        consts_loaded = sem("consts_loaded")
        gain0_loaded = sem("gain0_loaded")
        gain_loaded = [sem("gain_loaded0"), sem("gain_loaded1")]
        x_ready = sem("x_ready")
        xg_ready = sem("xg_ready")
        turned = sem("turned")
        a_hi_done = sem("a_hi_done")
        a_lo_done = sem("a_lo_done")
        ss_done = sem("ss_done")
        mean_done = sem("mean_done")
        power_done = sem("power_done")
        exponent_set = sem("exponent_set")
        chunk_done = sem("chunk_done")
        silu_done = sem("silu_done")
        chunk_out = sem("chunk_out")
        hid_turned = sem("hid_turned")
        h_hi_done = sem("h_hi_done")
        h_lo_done = sem("h_lo_done")
        acc_done = sem("acc_done")
        out_stored = sem("out_stored")
        step = sem("step")
        rows_loaded = sem("rows_loaded")
        rows_turned = sem("rows_turned")
        chan_set = sem("chan_set")
        tap_lo_set = sem("tap_lo_set")
        b_out_loaded = sem("b_out_loaded")
        up_lo_set = sem("up_lo_set")
        diag_hi_set = sem("diag_hi_set")
        diag_lo_set = sem("diag_lo_set")
        diag_used = sem("diag_used")
        cv_taken = sem("cv_taken")
        bin_loaded = [sem("bin_loaded0"), sem("bin_loaded1")]
        sig_done = sem("sig_done")
        ab_done = sem("ab_done")
        u_turned = sem("u_turned")
        pad_zero = sem("pad_zero")
        u_placed = sem("u_placed")
        tap_done = sem("tap_done")
        c_turned = sem("c_turned")
        ln_b_set = sem("ln_b_set")
        ln_done = [sem(f"ln_done{t}") for t in range(TT)]
        n_turned = sem("n_turned")
        act_done = sem("act_done")
        s_hi_done = sem("s_hi_done")
        s_lo_done = sem("s_lo_done")
        at_loaded = sem("at_loaded")
        lam_sum = sem("lam_sum")
        lam_exp = sem("lam_exp")
        qkv_out = sem("qkv_out")
        bias_set = sem("bias_set")
        o_placed = sem("o_placed")
        qn_done = sem("qn_done")
        q_turned = sem("q_turned")
        q_placed = sem("q_placed")
        sc_done = sem("sc_done")
        mx_done = sem("mx_done")
        ex_done = sem("ex_done")
        pr_done = sem("pr_done")
        p_turned = sem("p_turned")
        p_placed = sem("p_placed")
        o_done = sem("o_done")
        osq_done = sem("osq_done")
        on_done = sem("on_done")
        on_turned = sem("on_turned")
        o_hi_done = sem("o_hi_done")
        o_lo_done = sem("o_lo_done")

        block = ctx.enter_context(nc.Block())

        def over_taps(engine, pair, do, after_head=None):
            for j in range(HEAD):
                do(pair * W + j, j, 0)
            if after_head is not None:
                after_head()
            with engine.Fori(0, (W - HEAD - TAIL) // STEP) as i:
                for j in range(HEAD, HEAD + STEP):
                    do(pair * W + j, i * STEP + j, i)
            for j in range(W - TAIL, W):
                do(pair * W + j, j, 0)

        def w_in_source(s):
            kind, layer, which, _ = STAGES[s]
            if kind == "ffn":
                return ffn_w_in[layer, which].rearrange("(k p) n -> p k n", p=P), F
            if kind == "conv":
                return conv_w_in[0].rearrange("(k p) n -> p k n", p=P), D
            return attn_w_qkv[0].rearrange("(k p) n -> p k n", p=P), None

        def w_out_source(s):
            kind, layer, which, _ = STAGES[s]
            w = {"ffn": ffn_w_out[layer, which], "conv": conv_w_out[0], "attn": attn_w_out[0]}[kind]
            return w.rearrange("(k p) n -> p k n", p=P)

        @block.sync
        def _(sp):
            def slot_free(n, i):
                if n >= RAW:
                    sp.wait_ge(lo_done, 2 * (n - RAW + 1) + i * 2 * RING)

            def load_first(s, n, c, part, i=0):
                slot_free(n, i)
                src, apart = w_in_source(s)
                dst = raw[n % RAW][:].rearrange("p (k n) -> p k n", k=4)
                rows = slice(4 * part, 4 * part + 4)
                for g in range(2):
                    if apart is not None:
                        sp.dma_start(dst[:, :, g * CH:(g + 1) * CH],
                                     src[:, rows, bass.ds(c * CH + g * apart, CH)]).then_inc(raw_ready[n % RAW], 16)
                    else:
                        two = slice(4 * part + 2 * g, 4 * part + 2 * g + 2)
                        sp.dma_start(dst[:, 2 * g:2 * g + 2, :],
                                     src[:, two, bass.ds(QKV_CHUNKS[c] * BANK, BANK)]).then_inc(raw_ready[n % RAW], 16)

            def load_second(s, n, c, i=0):
                slot_free(n, i)
                src = w_out_source(s)
                dst = raw[n % RAW][:].rearrange("p (k n) -> p k n", k=2)
                for g in range(2):
                    sp.dma_start(dst[:, g:g + 1, :], src[:, bass.ds(c * 2 + g, 1), :]).then_inc(raw_ready[n % RAW], 16)

            for t in range(TT):
                sp.dma_start(xs[:, t, :], x[0, t * P:(t + 1) * P, :]).then_inc(x_loaded[t], 16)
            for s, (kind, _, _, chunks) in enumerate(STAGES):
                u = UNIT0[s]
                if kind == "ffn":
                    load_first(s, u, 0, 0)
                    load_first(s, u + 1, 0, 1)

                    def chunk(c, i):
                        n = u + 2 + 3 * (c - 1)
                        load_first(s, n, i * 2 + c, 0, i)
                        load_first(s, n + 1, i * 2 + c, 1, i)
                        load_second(s, n + 2, i * 2 + (c - 1), i)

                    chunk(1, 0)
                    chunk(2, 0)
                    with sp.Fori(0, (FCH - 3) // 2) as i:
                        chunk(3, i)
                        chunk(4, i)
                    load_second(s, u + 32, FCH - 1)
                else:
                    for c in range(chunks):
                        load_first(s, u + 2 * c, c, 0)
                        load_first(s, u + 2 * c + 1, c, 1)
                    for c in range(KT // 2):
                        load_second(s, u + 2 * chunks + c, c)
            for half in range(2):
                for t in range(TT):
                    sp.wait_ge(x_ready, 4 * 5 + 2 * half + t + 1)
                    sp.dma_start(out[0, t * P:(t + 1) * P, half * BANK:(half + 1) * BANK],
                                 xs[:, t, half * BANK:(half + 1) * BANK]).then_inc(out_stored, 16)
            sp.wait_ge(out_stored, 16 * 4)

        @block.gpsimd
        def _(pool):
            gains = [ffn_norm[0, 0], mix_norm[0], ffn_norm[0, 1], ffn_norm[1, 0], mix_norm[1], ffn_norm[1, 1]]
            def load_gain(n):
                pool.dma_start(gain[:, n % 2, :], gains[n].partition_broadcast(P)).then_inc(gain_loaded[n % 2], 16)

            pool.wait_ge(x_loaded[TT - 1], 16)
            load_gain(1)
            pool.dma_start(rows[0:W, :], conv_dw[0]).then_inc(rows_loaded, 16)
            for a, v in enumerate((conv_dw_b, conv_ln_g, conv_ln_b)):
                pool.dma_start(rows[W + a:W + a + 1, :], v).then_inc(rows_loaded, 16)
            pool.dma_start(b_out, conv_b_out[0].partition_broadcast(P)).then_inc(b_out_loaded, 16)
            nc.gpsimd.memset(up[:, :, 0:PAD], 0.0).then_inc(pad_zero, 1)
            nc.gpsimd.memset(exponent[:, :], -0.5).then_inc(exponent_set, 1)
            pool.wait_ge(exponent_set, 1)
            for n, (kind, a, t) in enumerate(POWERS):
                src, dst = {"turn": lambda: (msq[:, a, :], rstd[:, a, :]), "ln": lambda: (ln_v, ln_r),
                            "qk": lambda: (grp[:, t, :], grr[:, t, :]), "out": lambda: (grp[:, t, 0:GROUP], grr[:, t, 0:GROUP])}[kind]()
                if kind == "turn" and a == CONV:
                    for half in range(2):
                        pool.wait_ge(turned, 4 * CONV + 2 * half + 2)
                        cols = slice(half * BANK, (half + 1) * BANK)
                        pool.dma_start(b_in[:, :, cols], conv_b_in[0].rearrange("(g n) -> g n", g=2)[:, cols]
                                       .partition_broadcast(P)).then_inc(bin_loaded[half], 16)
                pool.wait_ge(mean_done, n + 1)
                nc.gpsimd.tensor_tensor(dst, src, exponent[:, 0:src.shape[-1]], ALU.pow).then_inc(power_done, 1)
                if kind == "turn" and a < 4:
                    pool.wait_ge(xg_ready, 4 * (a + 1))
                    load_gain(a + 2)
                if kind == "turn" and a == CONV:
                    pool.wait_ge(tap_lo_set, 1)

                    def lower(n, j, i):
                        if n >= SLOTS:
                            pool.wait_ge(diag_used, n - SLOTS + 1 + i * STEP)
                        for b in range(2):
                            mm = nc.gpsimd.tensor_tensor(diag(1, 2 * n + b), ident,
                                                         tap_lo[:, 2 * (n // W) + b, bass.ds(j, 1)].to_broadcast([P, P]),
                                                         ALU.mult)
                        mm.then_inc(diag_lo_set, 1)

                    pool.wait_ge(acc_done, 4 * CONV)
                    pool.wait_ge(pad_zero, 1)
                    for padded in (up_hi, up_lo):
                        nc.gpsimd.tensor_copy(padded[:, :, 0:PAD], up[:, 0:2, 0:PAD]).then_inc(pad_zero, 1)
                    for pair in range(PK // 2):
                        over_taps(pool, pair, lower)
                if kind == "turn" and a == CONV + 1:
                    pool.wait_ge(x_ready, 4 * (CONV + 1))
                    with nc.allow_non_contiguous_dma(reason="per-feature vectors, once"):
                        for c in range(2):
                            for b, v in enumerate((attn_q_norm, attn_k_norm)):
                                pool.dma_start(gq[c * DH:(c + 1) * DH, b:b + 1],
                                               v[0].rearrange("(d a) -> d a", a=1)).then_inc(at_loaded, 16)
                        pool.dma_start(gs, attn_subln_g[0].rearrange("(d a) -> d a", a=1)).then_inc(at_loaded, 16)
                    for b, v in enumerate((attn_lq1, attn_lk1, attn_lq2, attn_lk2)):
                        pool.dma_start(lam4[:, b, :], v[0].partition_broadcast(P)).then_inc(at_loaded, 16)

        @block.tensor
        def _(pe):
            def unit_ready(n, i=0):
                pe.wait_ge(lo_done, 2 * (n + 1) + i * 2 * RING)

            def products(dst, stat_hi, stat_lo, moves, first, last, begins, ends=None):
                for j, (m_hi, _) in enumerate(moves):
                    mm = pe.matmul(dst[j], stat_hi, m_hi, start=first, stop=False)
                    if begins and j == 0:
                        mm.then_inc(unit_begun, 1)
                for j, (_, m_lo) in enumerate(moves):
                    pe.matmul(dst[j], stat_hi, m_lo, start=False, stop=False)
                for j, (m_hi, _) in enumerate(moves):
                    mm = pe.matmul(dst[j], stat_lo, m_hi, start=False, stop=last)
                    if ends is not None:
                        mm.then_inc(ends, 1)

            def first_unit(n, part, banks, hooks={}, i=0, norm=None):
                if n:
                    unit_ready(n, i)
                else:
                    pe.wait_ge(lo_done, 1)
                hi, lo = w_hi[n % RING], w_lo[n % RING]
                pieces = [(k, t) for k in range(4) for t in range(TT)]
                if norm is not None:
                    pieces.sort(key=lambda piece: piece[1])
                for j, (k, t) in enumerate(pieces):
                    if j in hooks:
                        hooks[j]()
                    if norm is not None and k == 0:
                        pe.wait_ge(a_lo_done, 4 * norm + 2 * part + t + 1)
                    if n == 0 and j == 2:
                        unit_ready(n)
                    kt = 4 * part + k
                    cols = slice(k * BANK, (k + 1) * BANK)
                    tok = slice(t * P, (t + 1) * P)
                    end = kt == KT - 1
                    products([banks[t]], a_hi[:, kt, tok], a_lo[:, kt, tok], [(hi[:, cols], lo[:, cols])],
                             kt == 0, end, j == 0, chunk_done if end else None)

            def second_unit(s, n, left, first, last, hooks={}, i=0, by_tile=False):
                unit_ready(n, i)
                hi, lo = w_hi[n % RING], w_lo[n % RING]

                def part(k, t, halves, end, begins):
                    s_hi, s_lo = left(k)
                    tok = slice(t * P, (t + 1) * P)
                    moves = [(hi[:, k * D + h * BANK:k * D + (h + 1) * BANK],
                              lo[:, k * D + h * BANK:k * D + (h + 1) * BANK]) for h in halves]
                    products([acc[:, 2 * t + h, :] for h in halves], s_hi[:, tok], s_lo[:, tok], moves,
                             first and k == 0, end, begins, acc_done if end else None)

                if last:
                    for h in range(2):
                        for t in range(TT):
                            if h == t == 1 and s + 1 < len(STAGES):
                                turn(s + 1, 0, 0)
                            for k in range(2):
                                part(k, t, (h,), k == 1, h == t == k == 0)
                else:
                    pieces = [(k, t) for k in range(2) for t in range(TT)]
                    if by_tile:
                        pieces.sort(key=lambda piece: piece[1])
                    for j, (k, t) in enumerate(pieces):
                        if j in hooks:
                            hooks[j]()
                        part(k, t, (0, 1), False, j == 0)

            def turn(r, half, t):
                pe.wait_ge(xg_ready, 4 * r + 2 * half + t + 1)
                if half:
                    pe.wait_ge(a_lo_done, 4 * r + t + 1)
                for k in range(4):
                    mm = pe.transpose(pt[:, t, k * P:(k + 1) * P],
                                      xg[:, t, half * BANK + k * P:half * BANK + (k + 1) * P], ident)
                mm.then_inc(turned, 1)

            def enter(s, banks, extra=None):
                turn(s, 0, 1)
                first_unit(UNIT0[s], 0, banks, {5: lambda: turn(s, 1, 0), 6: lambda: turn(s, 1, 1)}, norm=s)
                first_unit(UNIT0[s] + 1, 1, banks, {0: extra} if extra is not None else {}, norm=s)

            def turn_rows():
                pe.wait_ge(rows_loaded, 16 * 4)
                for k in range(KT):
                    mm = pe.transpose(acc[:, 3, k * ROWS:(k + 1) * ROWS], rows[:, k * P:(k + 1) * P], ident[0:ROWS, 0:ROWS])
                mm.then_inc(rows_turned, 1)

            def ffn(s):
                f, u, o0 = FFN0[s], UNIT0[s], OUT0[s]
                banks = [pg[:, t, :] for t in range(TT)]
                banks0 = [acc[:, 2 * t, :] for t in range(TT)]

                def turn_hidden(c, i=0):
                    pe.wait_ge(chunk_out, 2 * (o0 + c + 1) + i * 4)
                    for k in range(2):
                        for t in range(TT):
                            mm = pe.transpose(pt[:, 0, (2 * k + t) * P:(2 * k + t + 1) * P],
                                              hid[:, t, k * P:(k + 1) * P], ident)
                    mm.then_inc(hid_turned, 1)

                def hidden_ready(c, i=0):
                    pe.wait_ge(h_lo_done, FCH * f + c + 1 + i * 2)

                def left(slot):
                    return lambda k: (h_hi[:, slot, k, :], h_lo[:, slot, k, :])

                enter(s, banks0, turn_rows if s == 0 else None)

                def chunk(c, b, i, first):
                    if c > 1:
                        pe.wait_ge(chunk_out, 2 * (o0 + c) + i * 4)
                    n = u + 2 + 3 * (c - 1)
                    first_unit(n, 0, banks, {4: lambda: turn_hidden(c - 1, 0)} if first else {}, i)
                    first_unit(n + 1, 1, banks, {}, i)
                    hidden_ready(c - 1, i)
                    second_unit(s, n + 2, left((c - 1) % 2), first, False, {2: lambda: turn_hidden(c, i)}, i)

                chunk(1, 1, 0, True)
                chunk(2, 0, 0, False)
                with pe.Fori(0, (FCH - 3) // 2) as i:
                    chunk(3, 1, i, False)
                    chunk(4, 0, i, False)
                hidden_ready(FCH - 1)
                second_unit(s, u + 32, left((FCH - 1) % 2), False, True)

            def a_left(w):
                return lambda k: (a_hi[:, 2 * w + k, :], a_lo[:, 2 * w + k, :])

            def conv(s):
                u, c0 = UNIT0[s], CHUNK0[s]
                chunks = STAGES[s][3]

                def turn_u(c):
                    pe.wait_ge(chunk_out, 2 * (c0 + c + 1))
                    if c >= 2:
                        pe.wait_ge(u_placed, c - 1)
                    for k in range(2):
                        for t in range(TT):
                            mm = pe.transpose(pt[:, c % 2, (2 * k + t) * P:(2 * k + t + 1) * P],
                                              hid[:, t, k * P:(k + 1) * P], ident)
                    mm.then_inc(u_turned, 1)

                for c in range(chunks):
                    banks = [(acc if c % 2 else pg)[:, t, :] for t in range(TT)]
                    if c >= 2:
                        pe.wait_ge(chunk_out, 2 * (c0 + c - 1))
                    if c == 0:
                        enter(s, banks)
                    else:
                        first_unit(u + 2 * c, 0, banks, {4: lambda: turn_u(c - 1)})
                        first_unit(u + 2 * c + 1, 1, banks)
                for pair in range(PK // 2):
                    first = chunks - PK // 2 + pair
                    if pair:
                        pe.wait_ge(u_placed, first + 1)
                    pe.wait_ge(up_lo_set, pair + 1)
                    pe.wait_ge(pad_zero, 3)

                    def shifted(n, j, i):
                        pe.wait_ge(diag_hi_set, n + 1 + i * STEP)
                        pe.wait_ge(diag_lo_set, n + 1 + i * STEP)
                        begins, ends = n % W == 0, n % W == W - 1
                        for b in range(2):
                            dst = acc[:, 2 - 2 * pair + b, 0:T]
                            d_hi, d_lo = diag(0, 2 * n + b), diag(1, 2 * n + b)
                            u_hi, u_lo = up_hi[:, b, bass.ds(j, T)], up_lo[:, b, bass.ds(j, T)]
                            pe.matmul(dst, d_hi, u_hi, start=begins, stop=False)
                            pe.matmul(dst, d_hi, u_lo, start=False, stop=False)
                            mm = pe.matmul(dst, d_lo, u_hi, start=False, stop=ends)
                        mm.then_inc(diag_used, 1)

                    over_taps(pe, pair, shifted, (lambda: turn_u(chunks - 1)) if pair == 0 else None)
                for k0, k1 in ((4, 6), (0, 4), (6, 8)):
                    for t, banks in enumerate((pg, pt)):
                        for k in range(k0, k1):
                            a = k // 4
                            if t == 0 and k % 2 == 0:
                                if k < VK:
                                    pe.wait_ge(tap_done, W * (k + 2))
                                else:
                                    pe.wait_ge(cv_taken, k - VK + 2)
                            mm = pe.transpose(banks[:, a, (k % 4) * P:(k % 4 + 1) * P], cv[:, k, t * P:(t + 1) * P], ident)
                        if k0 != 4:
                            mm.then_inc(c_turned, 1)
                for j in range(KT // 2):
                    for t in range(TT):
                        pe.wait_ge(ln_done[t], j // 2 + 1)
                        for k in range(2):
                            mm = pe.transpose((pt if j % 2 else pg)[:, j // 2, k * T + t * P:k * T + (t + 1) * P],
                                              xg[:, t, (2 * j + k) * P:(2 * j + k + 1) * P], ident)
                    mm.then_inc(n_turned, 1)
                for w in range(KT // 2):
                    pe.wait_ge(s_lo_done, w + 1)
                    second_unit(s, u + 2 * chunks + w, a_left(w), w == 0, w == KT // 2 - 1)

            def attn(s):
                u = UNIT0[s]
                reads = ({}, {})

                def pt_free(bank):
                    for name, reader in (("q", q_placed), ("p", p_placed), ("v", o_placed), ("o", o_lo_done)):
                        if name in reads[bank]:
                            pe.wait_ge(reader, reads[bank][name])

                def turn_q(m, t):
                    pe.wait_ge(qn_done, TT * m + t + 1)
                    pt_free(t)
                    for k in range(GROUP):
                        mm = pe.transpose(pt[:, t, k * P:(k + 1) * P],
                                          xg[:, 0, t * BANK + k * P:t * BANK + (k + 1) * P], ident)
                    mm.then_inc(q_turned, 1)
                    reads[t]["q"] = TT * m + t + 1

                def scores(n):
                    h, t = divmod(n, TT)
                    keys = (t + 1) * P
                    if h % GROUP == 0 and t == 0:
                        pe.wait_ge(q_placed, 4 * (h // GROUP + 1))
                    if n == GROUP * TT:
                        pe.wait_ge(qkv_out, 2 * (Q_OR_K[3] + 1))
                    if n >= 1:
                        pe.wait_ge(mx_done, n)
                    for c in range(2):
                        d = slice(c * DH, (c + 1) * DH)
                        mm = pe.matmul(score_banks(n)[:, c, 0:keys], qT[d, h, t * P:(t + 1) * P],
                                       kT[d, h, 0:keys], start=True, stop=True)
                    mm.then_inc(sc_done, 1)

                def turn_p(n):
                    pe.wait_ge(pr_done, n + 1)
                    pt_free(0)
                    for b in range(n % TT + 1):
                        mm = pe.transpose(pt[:, 0, b * P:(b + 1) * P], sc[:, n % 2, 0, b * P:(b + 1) * P], ident)
                    mm.then_inc(p_turned, 1)
                    reads[0]["p"] = n + 1

                def values(n):
                    h, t = divmod(n, TT)
                    pe.wait_ge(p_placed, n + 1)
                    pe.wait_ge(qkv_out, 2 * 3 * (h // GROUP + 1))
                    pt_free(1)
                    for b in range(t + 1):
                        mm = pe.matmul(pt[:, 1, 0:P], aT[:, n % 2, b, :], vv[:, b, h * P:(h + 1) * P],
                                       start=b == 0, stop=b == t)
                    mm.then_inc(o_done, 1)
                    reads[1]["v"] = n + 1

                def turn_o(g, t):
                    pe.wait_ge(on_done, TT * g + t + 1)
                    pt_free(t)
                    for k in range(GROUP):
                        mm = pe.transpose(pt[:, t, k * P:(k + 1) * P], o_sb[:, t, k * P:(k + 1) * P], ident)
                    mm.then_inc(on_turned, 1)
                    reads[t]["o"] = TT * g + t + 1

                def step(n):
                    if 0 <= n - 3 < STEPS:
                        values(n - 3)
                    if n < STEPS:
                        scores(n)
                    if 0 <= n - 2 < STEPS:
                        turn_p(n - 2)

                def between():
                    values(5)
                    turn_p(6)

                def step8():
                    values(6)
                    scores(8)
                    turn_p(7)

                def step9():
                    values(7)
                    scores(9)

                def step10():
                    scores(10)
                    turn_p(8)

                hooks = {(3, 2): lambda: turn_q(0, 0), (3, 5): lambda: turn_q(0, 1),
                         (5, 0): lambda: turn_q(1, 0), (5, 2): lambda: turn_q(1, 1),
                         (5, 5): lambda: step(0), (6, 2): lambda: step(1), (6, 7): lambda: step(2),
                         (7, 4): lambda: step(3), (8, 1): lambda: step(4), (8, 6): lambda: step(5),
                         (9, 3): lambda: step(6), (9, 6): lambda: turn_q(2, 0), (10, 0): lambda: turn_q(2, 1),
                         (10, 2): lambda: step(7), (10, 5): between,
                         (10, 7): lambda: turn_q(3, 0), (11, 0): lambda: turn_q(3, 1), (11, 2): step8, (11, 4): step9, (11, 6): step10}
                for c in range(6):
                    banks = [(acc[:, 2 + t, :] if c % 2 else pg[:, t, :]) for t in range(TT)]
                    if c >= 2:
                        pe.wait_ge(qkv_out, 2 * (c - 1))
                    if c == 0:
                        enter(s, banks)
                        continue
                    for part in range(2):
                        first_unit(u + 2 * c + part, part, banks,
                                   {at: do for (unit, at), do in hooks.items() if unit == 2 * c + part})
                turn_o(0, 0)
                turn_o(0, 1)
                scores(11)
                values(8)
                turn_p(9)
                pe.wait_ge(o_lo_done, 2)
                pe.wait_ge(qkv_out, 2 * 6)
                second_unit(s, u + 12, a_left(0), True, False,
                            {0: lambda: step(12), 1: lambda: step(13), 2: lambda: step(14), 3: lambda: step(15)})
                second_unit(s, u + 13, a_left(1), False, False,
                            {0: lambda: step(16), 1: lambda: step(17), 2: lambda: step(18), 3: lambda: turn_o(1, 0)})
                pe.wait_ge(o_lo_done, 3)
                second_unit(s, u + 14, a_left(2), False, False,
                            {1: lambda: turn_o(1, 1), 2: lambda: pe.wait_ge(o_lo_done, 4)}, by_tile=True)
                second_unit(s, u + 15, a_left(3), False, True)

            pe.wait_ge(consts_loaded, 16)
            turn(0, 0, 0)
            for s, (kind, _, _, _) in enumerate(STAGES):
                {"ffn": ffn, "conv": conv, "attn": attn}[kind](s)

        @block.scalar
        def _(act):
            def round_half(n, half, i=0):
                if half == 0:
                    act.wait_ge(raw_ready[n % RAW], 32 * (n // RAW + 1) + i * (32 * RING // RAW))
                    if n >= RING:
                        act.wait_ge(unit_begun, n - RING + 2 + i * RING)
                cols = slice(half * HALF, (half + 1) * HALF)
                nc.scalar.copy(w_hi[n % RING][:, cols], raw[n % RAW][:, cols]).then_inc(hi_done, 1)

            def tick(n, i=0, mid=None):
                if n + AHEAD < UNITS:
                    round_half(n + AHEAD, 0, i)
                if mid is not None:
                    mid()
                if n + AHEAD < UNITS:
                    round_half(n + AHEAD, 1, i)

            def turn(r, half, t):
                act.wait_ge(turned, 4 * r + 2 * half + t + 1)
                nc.scalar.copy(a_hi[:, 4 * half:4 * half + 4, t * P:(t + 1) * P],
                               pt[:, t, :].rearrange("p (k n) -> p k n", k=4)).then_inc(a_hi_done, 1)

            def square(r, half, t):
                if r == 0:
                    act.wait_ge(x_loaded[t], 16)
                else:
                    act.wait_ge(x_ready, 4 * (r - 1) + 2 * half + t + 1)
                if 4 * r + 2 * half + t >= 2:
                    act.wait_ge(ss_done, 4 * r + 2 * half + t - 1)
                nc.scalar.activation(junk[:, t, :], xs[:, t, half * BANK:(half + 1) * BANK], ACT.Square,
                                     accum_out=ss[:, r, t, half:half + 1]).then_inc(ss_done, 1)

            def enter(s):
                n = UNIT0[s] + AHEAD
                for half in range(2):
                    for t in range(TT):
                        turn(s, half, t)
                    for t in range(TT):
                        square(s, half, t)
                    round_half(n, half)

            def ffn(s):
                f, u, c0 = FFN0[s], UNIT0[s], CHUNK0[s]

                def gate(c, i=0):
                    for t in range(TT):
                        act.wait_ge(chunk_done, 2 * (c0 + c) + t + 1 + i * 4)
                        src = pg[:, t, 0:CH] if c else acc[:, 2 * t, 0:CH]
                        nc.scalar.activation(sil[:, t, :], src, ACT.Silu,
                                             scale=rstd[:, s, t:t + 1]).then_inc(silu_done, 1)

                def hidden(c, i=0):
                    act.wait_ge(hid_turned, FCH * f + c + 1 + i * 2)
                    nc.scalar.copy(h_hi[:, c % 2, :, :].rearrange("p k n -> p (k n)"), pt[:, 0, :]).then_inc(h_hi_done, 1)

                if s == 0:
                    for half in range(2):
                        for t in range(TT):
                            square(s, half, t)
                    for t in range(TT):
                        turn(s, 0, t)
                    for n in range(3):
                        round_half(n, 0)
                        round_half(n, 1)
                    for t in range(TT):
                        turn(s, 1, t)
                    round_half(3, 0)
                    round_half(3, 1)
                    tick(u)
                else:
                    enter(s)
                if s:
                    tick(u + 1)
                act.wait_ge(power_done, POWER_AT["turn", s, 0] + 1)
                gate(0)
                if s == 0:
                    act.wait_ge(rows_turned, 1)
                    nc.scalar.copy(chan[:].rearrange("p k w -> p (k w)"), acc[:, 3, 0:KT * ROWS]).then_inc(chan_set, 1)
                    act.wait_ge(chan_set, 1)
                    nc.scalar.copy(tap_hi, chan[:, VK:KT, 0:W]).then_inc(chan_set, 1)
                    tick(u + 1)
                tick(u + 2, 0, lambda: hidden(0))

                def chunk(c, i, skip_first):
                    n = u + 2 + 3 * (c - 1)
                    if not skip_first:
                        tick(n, i)
                    tick(n + 1, i)
                    gate(c, i)
                    tick(n + 2, i, lambda: hidden(c, i))

                chunk(1, 0, True)
                chunk(2, 0, False)
                peel = s == len(STAGES) - 1
                with act.Fori(0, (FCH - 3) // 2 - peel) as i:
                    chunk(3, i, False)
                    chunk(4, i, False)
                if peel:
                    chunk(FCH - 2, 0, False)
                    chunk(FCH - 1, 0, False)
                tick(u + 32)

            def conv(s):
                u, c0 = UNIT0[s], CHUNK0[s]
                chunks = STAGES[s][3]

                def place(c):
                    act.wait_ge(u_turned, c + 1)
                    dst = up[:, 2 * c:2 * c + 2, :] if 2 * c < VK else up_hi
                    if 2 * c > VK:
                        act.wait_ge(diag_used, W * (c - VK // 2))
                    nc.scalar.copy(dst[:, :, PAD:PAD + T],
                                   pt[:, c % 2, :].rearrange("p (k n) -> p k n", k=2)).then_inc(u_placed, 1)

                def sigmoids(c):
                    for t in range(TT):
                        act.wait_ge(ab_done, 2 * c + t + 1)
                        nc.scalar.activation(sg[:, t, :], ab[:, t, CH:2 * CH], ACT.Sigmoid).then_inc(sig_done, 1)

                def upper(n, j, i):
                    if n >= SLOTS:
                        act.wait_ge(diag_used, n - SLOTS + 1 + i * STEP)
                    for b in range(2):
                        mm = nc.scalar.activation(diag(0, 2 * n + b), ident, ACT.Copy,
                                                  scale=tap_hi[:, 2 * (n // W) + b, bass.ds(j, 1)].bitcast(F32))
                    mm.then_inc(diag_hi_set, 1)

                def take(pair):
                    act.wait_ge(diag_used, W * (pair + 1))
                    for b in range(2):
                        k = VK + 2 * pair + b
                        nc.scalar.activation(cv[:, k, :], acc[:, 2 - 2 * pair + b, 0:T], ACT.Identity,
                                             bias=chan[:, k, W:W + 1]).then_inc(cv_taken, 1)

                enter(s)
                for c in range(chunks):
                    if c:
                        tick(u + 2 * c, 0, lambda: place(c - 1))
                    tick(u + 2 * c + 1)
                    if c < chunks - 1:
                        sigmoids(c)
                over_taps(act, 0, upper, lambda: sigmoids(chunks - 1))
                place(chunks - 1)
                over_taps(act, 1, upper, lambda: take(0))
                take(1)
                nc.scalar.activation(warm, chan[:, 0, 0:1], ACT.Silu)
                act.wait_ge(power_done, POWER_AT["ln", 0, 0] + 1)
                act.wait_ge(ln_b_set, 1)
                for a in range(2):
                    nc.scalar.activation(xg[:, 1, a * BANK:(a + 1) * BANK], pt[:, a, :], ACT.Identity,
                                         bias=ln_b, scale=ln_r[:, 1:2]).then_inc(ln_done[1], 1)
                for j in range(KT // 2):
                    act.wait_ge(n_turned, j + 1)
                    for k in range(2):
                        kt = 2 * j + k
                        mm = nc.scalar.activation(cv[:, kt, :], (pt if j % 2 else pg)[:, j // 2, k * T:(k + 1) * T], ACT.Silu,
                                                  bias=chan[:, kt, W + 2:W + 3], scale=chan[:, kt, W + 1:W + 2])
                    mm.then_inc(act_done, 1)
                    act.wait_ge(act_done, j + 1)
                    nc.scalar.copy(a_hi[:, 2 * j:2 * j + 2, :], cv[:, 2 * j:2 * j + 2, :]).then_inc(s_hi_done, 1)
                tick(u + 2 * chunks)
                for w in range(1, 4):
                    tick(u + 2 * chunks + w)

            def attn(s):
                u, c0 = UNIT0[s], CHUNK0[s]

                def take(c):
                    for t in range(TT):
                        act.wait_ge(chunk_done, 2 * (c0 + c) + t + 1)
                        src = acc[:, 2 + t, :] if c % 2 else pg[:, t, :]
                        if c not in Q_OR_K:
                            nc.scalar.activation(vv[:, t, (c // 3) * BANK:(c // 3 + 1) * BANK], src, ACT.Copy,
                                                 scale=rstd[:, s, t:t + 1]).then_inc(qkv_out, 1)
                            continue
                        m = Q_OR_K.index(c)
                        if m and t == 0:
                            act.wait_ge(q_turned, TT * m)
                        nc.scalar.activation(xg[:, 0, t * BANK:(t + 1) * BANK], src, ACT.Copy,
                                             scale=rstd[:, s, t:t + 1])
                        nc.scalar.activation(xg[:, 1, t * BANK:(t + 1) * BANK], src, ACT.Square,
                                             scale=rstd[:, s, t:t + 1]).then_inc(qkv_out, 1)

                def place_q(m):
                    dst, a = (qT, 0) if m % 2 == 0 else (kT, 1)
                    if m == 0:
                        act.wait_ge(at_loaded, 16 * 9)
                    for t in range(TT):
                        act.wait_ge(q_turned, 2 * m + t + 1)
                        nc.scalar.activation(dst[:, GROUP * (m // 2):GROUP * (m // 2 + 1), t * P:(t + 1) * P],
                                             pt[:, t, :].rearrange("p (k n) -> p k n", k=4), ACT.Copy,
                                             scale=gq[:, a:a + 1]).then_inc(q_placed, 1)

                def set_bias(h):
                    if h >= 2:
                        act.wait_ge(mx_done, 2 * h - 2)
                    nc.scalar.activation(bias[:, h % 2, :], dist, ACT.Copy, scale=-2.0 ** (-8.0 * (h + 1) / H)).then_inc(bias_set, 1)

                def exps(n):
                    keys = (n % TT + 1) * P
                    act.wait_ge(mx_done, n + 1)
                    for c in range(2):
                        mm = nc.scalar.activation(sc[:, n % 2, c, 0:keys], sc[:, n % 2, c, 0:keys], ACT.Exp, scale=-1.0,
                                                  bias=mx[:, n % 2, c:c + 1], accum_out=sm[:, n % 2, c:c + 1])
                    mm.then_inc(ex_done, 1)

                def place_p(n):
                    keys = (n % TT + 1) * P
                    act.wait_ge(p_turned, n + 1)
                    if n >= 2:
                        act.wait_ge(o_done, n - 1)
                    nc.scalar.copy(aT[:, n % 2, :, :].rearrange("p b n -> p (b n)")[:, 0:keys],
                                   pt[:, 0, 0:keys]).then_inc(p_placed, 1)

                def place_o(n):
                    h, t = divmod(n, TT)
                    act.wait_ge(o_done, n + 1)
                    k = h % GROUP
                    nc.scalar.activation(o_sb[:, t, k * P:(k + 1) * P], pt[:, 1, 0:P], ACT.Copy,
                                         scale=rs[:, n % 4, 0:1]).then_inc(o_placed, 1)

                def squares(g, t):
                    act.wait_ge(o_placed, TT * (GROUP * (g + 1) - 1) + t + 1)
                    nc.scalar.activation(xg[:, 1, t * BANK:(t + 1) * BANK], o_sb[:, t, :], ACT.Square).then_inc(osq_done, 1)

                def round_o(g, t):
                    act.wait_ge(on_turned, TT * g + t + 1)
                    nc.scalar.activation(a_hi[:, GROUP * g:GROUP * (g + 1), t * P:(t + 1) * P],
                                         pt[:, t, :].rearrange("p (k n) -> p k n", k=4), ACT.Copy,
                                         scale=gs).then_inc(o_hi_done, 1)

                def step(n):
                    if 0 <= n - 3 < STEPS:
                        place_o(n - 3)
                    if 0 <= n - 2 < STEPS:
                        place_p(n - 2)
                    if n < STEPS:
                        exps(n)

                enter(s)
                tick(u + 1)
                act.wait_ge(lam_sum, 1)
                nc.scalar.activation(lsum, lsum, ACT.Exp).then_inc(lam_exp, 1)
                set_bias(0)
                set_bias(1)
                tick(u + 2)
                act.wait_ge(power_done, POWER_AT["turn", s, 0] + 1)
                take(0)
                tick(u + 3)
                place_q(0)
                tick(u + 4)
                take(1)
                tick(u + 5)
                place_q(1)
                tick(u + 6)
                step(0)
                take(2)
                step(1)
                tick(u + 7)
                step(2)
                set_bias(2)
                step(3)
                tick(u + 8)
                take(3)
                step(4)
                tick(u + 9)
                set_bias(3)
                step(5)
                tick(u + 10)
                step(6)
                place_q(2)
                take(4)
                step(7)
                place_o(5)
                place_p(6)
                set_bias(4)
                place_q(3)
                tick(u + 11)
                place_o(6)
                place_p(7)
                exps(8)
                place_o(7)
                squares(0, 0)
                squares(0, 1)
                exps(9)
                set_bias(5)
                place_p(8)
                take(5)
                round_o(0, 0)
                round_o(0, 1)
                exps(10)
                step(11)
                set_bias(6)
                step(12)
                tick(u + 12)
                step(13)
                set_bias(7)
                for n in range(14, STEPS + 2):
                    step(n)
                squares(1, 0)
                step(STEPS + 2)
                squares(1, 1)
                round_o(1, 0)
                tick(u + 13)
                round_o(1, 1)
                tick(u + 14)
                tick(u + 15)

            act.dma_start(gain[:, 0, :], ffn_norm[0, 0].partition_broadcast(P)).then_inc(gain0_loaded, 16)
            act.dma_start(consts[:, :], shape_consts).then_inc(consts_loaded, 16)
            for s, (kind, _, _, _) in enumerate(STAGES):
                {"ffn": ffn, "conv": conv, "attn": attn}[kind](s)

        @block.vector
        def _(dve):
            links = [0]

            def link(ins):
                links[0] += 1
                ins.then_inc(step, 1)
                dve.wait_ge(step, links[0])

            def power_ready(*key):
                dve.wait_ge(power_done, POWER_AT[key] + 1)

            def rest_half(n, half, i=0):
                dve.wait_ge(hi_done, 2 * n + half + 1 + i * 2 * RING)
                cols = slice(half * HALF, (half + 1) * HALF)
                nc.vector.tensor_tensor(w_lo[n % RING][:, cols], raw[n % RAW][:, cols],
                                        w_hi[n % RING][:, cols].bitcast(F32), ALU.subtract).then_inc(lo_done, 1)

            def tick(n, i=0, mid=None):
                if n + AHEAD < UNITS:
                    rest_half(n + AHEAD, 0, i)
                if mid is not None:
                    mid()
                if n + AHEAD < UNITS:
                    rest_half(n + AHEAD, 1, i)

            def update(r, half, t, scale):
                cols = slice(half * BANK, (half + 1) * BANK)
                dve.wait_ge(acc_done, 4 * (r - 1) + 2 * half + t + 1)
                nc.vector.scalar_tensor_tensor(out=xs[:, t, cols], in0=acc[:, 2 * t + half, :], scalar=scale,
                                               in1=xs[:, t, cols], op0=ALU.mult, op1=ALU.add).then_inc(x_ready, 1)

            def times_gain(r, half, t):
                cols = slice(half * BANK, (half + 1) * BANK)
                if r:
                    dve.wait_ge(x_ready, 4 * (r - 1) + 2 * half + t + 1)
                    dve.wait_ge(gain_loaded[r % 2], 16 * ((r + 1) // 2))
                else:
                    dve.wait_ge(x_loaded[t], 16)
                    dve.wait_ge(gain0_loaded, 16)
                nc.vector.tensor_tensor(xg[:, t, cols], xs[:, t, cols], gain[:, r % 2, cols], ALU.mult).then_inc(xg_ready, 1)

            def turn_rest(r, half, t):
                dve.wait_ge(a_hi_done, 4 * r + 2 * half + t + 1)
                dst = (slice(None), slice(4 * half, 4 * half + 4), slice(t * P, (t + 1) * P))
                nc.vector.tensor_tensor(a_lo[dst], pt[:, t, :].rearrange("p (k n) -> p k n", k=4),
                                        a_hi[dst].bitcast(F32), ALU.subtract).then_inc(a_lo_done, 1)

            def token_factors(r):
                dve.wait_ge(ss_done, 4 * (r + 1))
                link(nc.vector.tensor_tensor(msq[:, r, :], ss[:, r, :, 0], ss[:, r, :, 1], ALU.add))
                nc.vector.tensor_scalar(msq[:, r, :], msq[:, r, :], 1.0 / D, EPS, ALU.mult, ALU.add).then_inc(mean_done, 1)

            def enter(s, scale):
                if s == 0:
                    for half in range(2):
                        for t in range(TT):
                            times_gain(s, half, t)
                    for t in range(TT):
                        turn_rest(s, 0, t)
                    for n in range(3):
                        rest_half(n, 0)
                        rest_half(n, 1)
                    for t in range(TT):
                        turn_rest(s, 1, t)
                    token_factors(s)
                    rest_half(3, 0)
                    rest_half(3, 1)
                    tick(UNIT0[s])
                    return
                n = UNIT0[s] + AHEAD
                for t in range(TT):
                    update(s, 0, t, scale)
                    times_gain(s, 0, t)
                for t in range(TT):
                    update(s, 1, t, scale)
                    turn_rest(s, 0, t)
                    times_gain(s, 1, t)
                rest_half(n, 0)
                for t in range(TT):
                    turn_rest(s, 1, t)
                token_factors(s)
                rest_half(n, 1)

            def ffn(s):
                f, u, c0 = FFN0[s], UNIT0[s], CHUNK0[s]

                def gated(c, i=0):
                    for t in range(TT):
                        dve.wait_ge(silu_done, 2 * (FCH * f + c) + t + 1 + i * 4)
                        src = pg[:, t, CH:2 * CH] if c else acc[:, 2 * t, CH:2 * CH]
                        nc.vector.scalar_tensor_tensor(out=hid[:, t, :], in0=src,
                                                       scalar=rstd[:, s, t:t + 1], in1=sil[:, t, :],
                                                       op0=ALU.mult, op1=ALU.mult).then_inc(chunk_out, 1)

                def hidden(c, i=0):
                    dve.wait_ge(h_hi_done, FCH * f + c + 1 + i * 2)
                    nc.vector.tensor_tensor(h_lo[:, c % 2, :, :].rearrange("p k n -> p (k n)"), pt[:, 0, :],
                                            h_hi[:, c % 2, :, :].rearrange("p k n -> p (k n)").bitcast(F32),
                                            ALU.subtract).then_inc(h_lo_done, 1)

                if s:
                    tick(u + 1)
                power_ready("turn", s, 0)
                gated(0)
                if s == 0:
                    dve.wait_ge(chan_set, 2)
                    nc.vector.tensor_tensor(tap_lo, chan[:, VK:KT, 0:W], tap_hi.bitcast(F32), ALU.subtract).then_inc(tap_lo_set, 1)
                    tick(u + 1)
                tick(u + 2, 0, lambda: hidden(0))

                def chunk(c, i, skip_first):
                    n = u + 2 + 3 * (c - 1)
                    if not skip_first:
                        tick(n, i)
                    tick(n + 1, i)
                    gated(c, i)
                    tick(n + 2, i, lambda: hidden(c, i))

                chunk(1, 0, True)
                chunk(2, 0, False)
                peel = s == len(STAGES) - 1
                with dve.Fori(0, (FCH - 3) // 2 - peel) as i:
                    chunk(3, i, False)
                    chunk(4, i, False)
                if peel:
                    chunk(FCH - 2, 0, False)
                    chunk(FCH - 1, 0, False)
                tick(u + 32)

            def conv(s):
                u, c0 = UNIT0[s], CHUNK0[s]
                chunks = STAGES[s][3]

                def glu(c):
                    src = acc if c % 2 else pg
                    dve.wait_ge(bin_loaded[c * CH // BANK], 16)
                    for t in range(TT):
                        dve.wait_ge(chunk_done, 2 * (c0 + c) + t + 1)
                        nc.vector.scalar_tensor_tensor(
                            out=ab[:, t, :].rearrange("p (g n) -> p g n", g=2),
                            in0=src[:, t, :].rearrange("p (g n) -> p g n", g=2),
                            scalar=rstd[:, s, t:t + 1], in1=b_in[:, :, c * CH:(c + 1) * CH],
                            op0=ALU.mult, op1=ALU.add).then_inc(ab_done, 1)
                    for t in range(TT):
                        dve.wait_ge(sig_done, 2 * c + t + 1)
                        nc.vector.tensor_tensor(hid[:, t, :], ab[:, t, 0:CH], sg[:, t, :], ALU.mult).then_inc(chunk_out, 1)

                def first_tap(c):
                    dve.wait_ge(u_placed, c + 1)
                    for k in (2 * c, 2 * c + 1):
                        nc.vector.tensor_scalar(cv[:, k, :], up[:, k, 0:T], chan[:, k, 0:1], chan[:, k, W:W + 1],
                                                ALU.mult, ALU.add).then_inc(tap_done, 1)

                def more_taps(c, start, stop, step):
                    with dve.Fori(0, (stop - start) // step) as i:
                        for j in range(start, start + step):
                            for b, k in enumerate((2 * c, 2 * c + 1)):
                                dve.wait_ge(tap_done, 2 * (W * c + j - 1) + b + 1 + i * 2 * step)
                                nc.vector.scalar_tensor_tensor(
                                    out=cv[:, k, :], in0=up[:, k, bass.ds(i * step + j, T)],
                                    scalar=chan[:, k, bass.ds(i * step + j, 1)], in1=cv[:, k, :],
                                    op0=ALU.mult, op1=ALU.add).then_inc(tap_done, 1)

                def lower_input(c):
                    dve.wait_ge(u_placed, c + 1)
                    nc.vector.tensor_tensor(up_lo[:, :, PAD:PAD + T], pt[:, c % 2, :].rearrange("p (k n) -> p k n", k=2),
                                            up_hi[:, :, PAD:PAD + T].bitcast(F32), ALU.subtract).then_inc(up_lo_set, 1)

                dve.wait_ge(pad_zero, 1)
                power_ready("turn", s, 0)
                tick(u + 1)
                glu(0)
                tick(u + 2)
                tick(u + 3)
                glu(1)
                first_tap(0)
                more_taps(0, 1, 5, 2)
                tick(u + 4)
                tick(u + 5)
                glu(2)
                more_taps(0, 5, 9, 2)
                tick(u + 6)
                lower_input(2)
                tick(u + 7)
                glu(3)
                more_taps(0, 9, W - 2, 5)
                more_taps(0, W - 2, W, 1)
                first_tap(1)
                more_taps(1, 1, 3, 1)
                lower_input(3)
                more_taps(1, 3, W, 7)
                for a in range(2):
                    for t, banks in enumerate((pg, pt)):
                        dve.wait_ge(c_turned, 2 * a + t + 1)
                        mm = nc.vector.bn_stats(bn[:, t, a, :], banks[:, a, :])
                        if a == 1:
                            link(mm)
                            link(nc.vector.bn_aggr(mv[:, t, :], bn[:, t, :, :]))
                nc.vector.tensor_scalar(ln_v, mv[:, :, 1], EPS, None, ALU.add).then_inc(mean_done, 1)
                power_ready("ln", 0, 0)
                nc.vector.scalar_tensor_tensor(out=ln_b, in0=mv[:, 1, 0:1], scalar=-1.0, in1=ln_r[:, 1:2],
                                               op0=ALU.mult, op1=ALU.mult).then_inc(ln_b_set, 1)
                for a in range(2):
                    nc.vector.tensor_scalar(xg[:, 0, a * BANK:(a + 1) * BANK], pg[:, a, :],
                                            mv[:, 0, 0:1], ln_r[:, 0:1], ALU.subtract, ALU.mult).then_inc(ln_done[0], 1)
                for j in range(KT // 2):
                    dve.wait_ge(s_hi_done, j + 1)
                    nc.vector.tensor_tensor(a_lo[:, 2 * j:2 * j + 2, :], cv[:, 2 * j:2 * j + 2, :],
                                            a_hi[:, 2 * j:2 * j + 2, :].bitcast(F32), ALU.subtract).then_inc(s_lo_done, 1)
                dve.wait_ge(b_out_loaded, 16)
                tick(u + 2 * chunks)
                for t in range(TT):
                    mm = nc.vector.tensor_tensor(xs[:, t, :], xs[:, t, :], b_out, ALU.add)
                link(mm)
                for w in range(1, 4):
                    tick(u + 2 * chunks + w)

            def attn(s):
                u = UNIT0[s]

                def lambdas():
                    dve.wait_ge(at_loaded, 16 * 9)
                    for a in range(2):
                        link(nc.vector.tensor_tensor(lprod, lam4[:, 2 * a, :], lam4[:, 2 * a + 1, :], ALU.mult))
                        mm = nc.vector.reduce_sum(lsum[:, a:a + 1], lprod, AX_X)
                        if a == 0:
                            link(mm)
                    mm.then_inc(lam_sum, 1)

                def groups(src, t, n):
                    return src[:, t, :].rearrange("p (g d) -> p g d", d=n)

                def norm(scaled, t, n, power, done):
                    power_ready(*power)
                    g = BANK // n
                    factors = grr[:, t, 0:g].rearrange("p (g a) -> p g a", a=1).to_broadcast([P, g, n])
                    nc.vector.tensor_tensor(groups(scaled, t, n), groups(scaled, t, n), factors, ALU.mult).then_inc(done, 1)

                def mean_squares(t, n, under):
                    g = grp[:, t, 0:BANK // n]
                    link(nc.vector.reduce_sum(g, groups(halves(1), t, n), AX_X))
                    nc.vector.tensor_scalar(g, g, under / n, under * EPS, ALU.mult, ALU.add).then_inc(mean_done, 1)

                def halves(a):
                    return xg[:, a, :].rearrange("p (t n) -> p t n", t=TT)

                def norm_qk(m):
                    for t in range(TT):
                        dve.wait_ge(qkv_out, 2 * Q_OR_K[m] + t + 1)
                        mean_squares(t, DH, float(DH) if m % 2 == 0 else 1.0)
                    for t in range(TT):
                        norm(halves(0), t, DH, ("qk", m, t), qn_done)

                def norm_out(g, t):
                    dve.wait_ge(osq_done, TT * g + t + 1)
                    mean_squares(t, P, (1.0 - LAMBDA_INIT) ** -2)

                def biased(n):
                    h, t = divmod(n, TT)
                    keys = (t + 1) * P
                    dve.wait_ge(sc_done, n + 1)
                    dve.wait_ge(bias_set, h + 1)
                    if n >= 2:
                        dve.wait_ge(p_turned, n - 1)
                    for c in range(2):
                        mm = nc.vector.tensor_tensor_reduce(
                            sc[:, n % 2, c, 0:keys], score_banks(n)[:, c, 0:keys], bias[:, h % 2, 2 * P - keys:2 * P],
                            -1.0, HUGE, ALU.add, ALU.min, mx[:, n % 2, c:c + 1])
                    mm.then_inc(mx_done, 1)

                def combined(n):
                    keys = (n % TT + 1) * P
                    dve.wait_ge(ex_done, n + 1)
                    link(nc.vector.reciprocal(rs[:, n % 4, :], sm[:, n % 2, :]))
                    f = fac[:, n % 2:n % 2 + 1]
                    link(nc.vector.tensor_scalar(f, rs[:, n % 4, 1:2], sm[:, n % 2, 0:1], nlam, ALU.mult, ALU.mult))
                    nc.vector.scalar_tensor_tensor(out=sc[:, n % 2, 0, 0:keys], in0=sc[:, n % 2, 1, 0:keys],
                                                   scalar=f, in1=sc[:, n % 2, 0, 0:keys],
                                                   op0=ALU.mult, op1=ALU.add).then_inc(pr_done, 1)

                def rest_o(g, t):
                    dve.wait_ge(o_hi_done, TT * g + t + 1)
                    dst = (slice(None), slice(GROUP * g, GROUP * (g + 1)), slice(t * P, (t + 1) * P))
                    nc.vector.scalar_tensor_tensor(out=a_lo[dst], in0=pt[:, t, :].rearrange("p (k n) -> p k n", k=4),
                                                   scalar=gs, in1=a_hi[dst].bitcast(F32), op0=ALU.mult,
                                                   op1=ALU.subtract).then_inc(o_lo_done, 1)

                def step(n):
                    if n < STEPS:
                        biased(n)
                    combined(n - 1)

                lambdas()
                tick(u + 1)
                tick(u + 2)
                norm_qk(0)
                tick(u + 3)
                tick(u + 4)
                norm_qk(1)
                tick(u + 5)
                dve.wait_ge(lam_exp, 1)
                link(nc.vector.tensor_tensor(nlam, lsum[:, 1:2], lsum[:, 0:1], ALU.subtract))
                link(nc.vector.tensor_scalar(nlam, nlam, -LAMBDA_INIT, None, ALU.add))
                tick(u + 6)
                biased(0)
                step(1)
                tick(u + 7)
                step(2)
                step(3)
                tick(u + 8)
                step(4)
                tick(u + 9)
                step(5)
                norm_qk(2)
                step(6)
                tick(u + 10)
                combined(6)
                biased(7)
                norm_qk(3)
                combined(7)
                tick(u + 11)
                biased(8)
                step(9)
                norm_out(0, 0)
                norm_out(0, 1)
                for t in range(TT):
                    norm(o_sb, t, P, ("out", 0, t), on_done)
                step(10)
                rest_o(0, 0)
                rest_o(0, 1)
                step(11)
                step(12)
                tick(u + 12)
                for n in range(13, STEPS + 1):
                    step(n)
                norm_out(1, 0)
                norm(o_sb, 0, P, ("out", 1, 0), on_done)
                norm_out(1, 1)
                rest_o(1, 0)
                norm(o_sb, 1, P, ("out", 1, 1), on_done)
                tick(u + 13)
                rest_o(1, 1)
                tick(u + 14)
                tick(u + 15)

            for s, (kind, _, _, _) in enumerate(STAGES):
                enter(s, 0.5 if s and STAGES[s - 1][0] == "ffn" else 1.0)
                {"ffn": ffn, "conv": conv, "attn": attn}[kind](s)
            for half in range(2):
                for t in range(TT):
                    update(len(STAGES), half, t, 0.5)


NAMES = ["x", "ffn_norm", "ffn_w_in", "ffn_w_out", "mix_norm", "conv_w_in", "conv_b_in", "conv_dw", "conv_dw_b",
         "conv_ln_g", "conv_ln_b", "conv_w_out", "conv_b_out", "attn_w_qkv", "attn_q_norm", "attn_k_norm",
         "attn_lq1", "attn_lk1", "attn_lq2", "attn_lk2", "attn_subln_g", "attn_w_out"]


def kernel(**inputs):
    import concourse.bacc as bacc
    from concourse.bass_utils import run_bass_kernel_spmd as run

    nc = bacc.Bacc("TRN2", target_bir_lowering=False, num_devices=1)
    arrays, args = {}, []
    for name in NAMES:
        a = np.ascontiguousarray(inputs[name])
        arrays[f"in_{name}"] = a
        args.append(nc.dram_tensor(f"in_{name}", a.shape, mybir.dt.from_np(a.dtype), kind="ExternalInput").ap())
    away = np.arange(P)[:, None] + P - np.arange(2 * P)[None, :]
    consts = np.concatenate([np.eye(P), np.where(away < 0, FAR, away)], axis=1).astype(np.float32)
    arrays["in_consts"] = consts
    args.append(nc.dram_tensor("in_consts", consts.shape, F32, kind="ExternalInput").ap())
    y = nc.dram_tensor("out_y", (1, T, D), F32, kind="ExternalOutput").ap()
    trunk(nc, *args, y)
    return run(nc, [arrays], core_ids=[0]).results[0]["out_y"]
```
